# Optimizing a Trainium2 kernel written in Bass

```python
import math
import jax, jax.numpy as jnp
from jax import lax
import numpy as np

D_MODEL = 2048
BATCH = 1
SEQ = 256
DEPTH = 2

GRID_W = 64
CTX_LEN = 256
N_MIXERS = 2
N_LRU = (DEPTH + 1) // 2
N_ATT = DEPTH // 2
LRU_WIDTH = D_MODEL
LRU_BLOCKS = 16
LRU_BLOCK = LRU_WIDTH // LRU_BLOCKS
LRU_C = 8.0
CONV_W = 4
CONV_PAD = (2, 1)
ATT_HEAD_DIM = 64
ATT_HEADS = D_MODEL // (2 * ATT_HEAD_DIM)
ATT_V_DIM = 2 * ATT_HEAD_DIM
ATT_WIDTH = ATT_HEADS * ATT_V_DIM
ROPE_FREQS = ATT_HEAD_DIM // 4
ROPE_BASE = 10000.0
Q_BLOCK = 128
EPS = 1e-6


def rms_norm(x, g):
    xf = x.astype(jnp.float32)
    y = xf * lax.rsqrt(jnp.mean(xf * xf, axis=-1, keepdims=True) + EPS)
    return (y * g.astype(jnp.float32)).astype(x.dtype)

def dwconv(u, w, b):
    y = lax.conv_general_dilated(u, w[:, None, :], window_strides=(1,), padding=[CONV_PAD],
                                 dimension_numbers=("NWC", "WIO", "NWC"),
                                 feature_group_count=u.shape[-1])
    return y + b

def lru_coeffs(xc, gw, gb, lam):
    B_, L, _ = xc.shape
    xb = xc.reshape(B_, L, LRU_BLOCKS, LRU_BLOCK)
    gates = jax.nn.sigmoid((jnp.einsum("blnc,gncd->gblnd", xb, gw) + gb[:, None, None]).astype(jnp.float32))
    gates = gates.reshape(2, B_, L, LRU_WIDTH)
    r, i = gates[0], gates[1]
    log_a = -LRU_C * r * jax.nn.softplus(-lam.astype(jnp.float32))
    a = jnp.exp(log_a)
    b = jnp.sqrt(-jnp.expm1(2.0 * log_a)) * (i * xc.astype(jnp.float32))
    return a, b

def linear_scan(a, b, h0, reverse):
    def step(h, ab):
        at, bt = ab
        h = at * h + bt
        return h, h
    h_end, hs = lax.scan(step, h0, (jnp.swapaxes(a, 0, 1), jnp.swapaxes(b, 0, 1)), reverse=reverse)
    return h_end, jnp.swapaxes(hs, 0, 1)

def rglru_mixer(h_lat, h_ctx, w_in, conv_w, conv_b, gate_w, gate_b, lam, w_out, need_ctx_out):
    u_lat, g_lat = jnp.split(h_lat @ w_in, 2, axis=-1)
    u_ctx, g_ctx = jnp.split(h_ctx @ w_in, 2, axis=-1)
    xc_lat = dwconv(u_lat, conv_w, conv_b)
    xc_ctx = dwconv(u_ctx, conv_w, conv_b)
    h0 = jnp.zeros((h_lat.shape[0], LRU_WIDTH), jnp.float32)
    outs_lat, outs_ctx = [], []
    for d, rev in enumerate((False, True)):
        a_c, b_c = lru_coeffs(xc_ctx, gate_w[d], gate_b[d], lam[d])
        h_end, hs_ctx = linear_scan(a_c, b_c, h0, rev)
        a_l, b_l = lru_coeffs(xc_lat, gate_w[d], gate_b[d], lam[d])
        _, hs_lat = linear_scan(a_l, b_l, h_end, rev)
        outs_lat.append(hs_lat)
        outs_ctx.append(hs_ctx)
    y_lat = ((outs_lat[0] + outs_lat[1]).astype(h_lat.dtype) * jax.nn.silu(g_lat)) @ w_out
    y_ctx = None
    if need_ctx_out:
        y_ctx = ((outs_ctx[0] + outs_ctx[1]).astype(h_ctx.dtype) * jax.nn.silu(g_ctx)) @ w_out
    return y_lat, y_ctx

def axial_rope_tables(S):
    rows = S // GRID_W
    row = jnp.broadcast_to(jnp.arange(rows)[:, None], (rows, GRID_W)).reshape(S).astype(jnp.float32)
    col = jnp.broadcast_to(jnp.arange(GRID_W)[None, :], (rows, GRID_W)).reshape(S).astype(jnp.float32)
    inv = ROPE_BASE ** (-jnp.arange(ROPE_FREQS, dtype=jnp.float32) / ROPE_FREQS)
    ang = jnp.stack([row[:, None] * inv, col[:, None] * inv], axis=1)
    return jnp.cos(ang), jnp.sin(ang)

def apply_axial_rope(x, cos, sin):
    xs = x.astype(jnp.float32).reshape(x.shape[:-1] + (2, 2, ROPE_FREQS))
    x1, x2 = xs[..., 0, :], xs[..., 1, :]
    out = jnp.stack([x1 * cos - x2 * sin, x2 * cos + x1 * sin], axis=-2)
    return out.reshape(x.shape).astype(x.dtype)

def diff_attend(q, k, v, lam):
    s = jnp.einsum("bhcqd,bhckd->bhcqk", q, k).astype(jnp.float32)
    p = jax.nn.softmax(s, axis=-1)
    attn = p[:, :, 0] - lam * p[:, :, 1]
    return jnp.einsum("bhqk,bhkv->bhqv", attn.astype(v.dtype), v)

def diff_attn_mixer(h_lat, h_ctx, w_in, q_g, k_g, lam_vecs, subln_g, w_out, lam_init, cos, sin, need_ctx_out):
    def project(h):
        B_, L, _ = h.shape
        q, k, v, g = jnp.split(h @ w_in, 4, axis=-1)
        q = rms_norm(q.reshape(B_, L, ATT_HEADS, 2, ATT_HEAD_DIM), q_g).transpose(0, 2, 3, 1, 4)
        k = rms_norm(k.reshape(B_, L, ATT_HEADS, 2, ATT_HEAD_DIM), k_g).transpose(0, 2, 3, 1, 4)
        v = v.reshape(B_, L, ATT_HEADS, ATT_V_DIM).transpose(0, 2, 1, 3)
        return q * (ATT_HEAD_DIM ** -0.5), k, v, g

    def finish(o, g):
        B_, _, L, _ = o.shape
        o = rms_norm(o, subln_g) * (1.0 - lam_init)
        o = o.transpose(0, 2, 1, 3).reshape(B_, L, ATT_WIDTH)
        return (o * jax.nn.silu(g)) @ w_out

    lv = lam_vecs.astype(jnp.float32)
    lam = jnp.exp(jnp.sum(lv[0] * lv[1])) - jnp.exp(jnp.sum(lv[2] * lv[3])) + lam_init

    q_l, k_l, v_l, g_l = project(h_lat)
    q_c, k_c, v_c, g_c = project(h_ctx)
    q_l = apply_axial_rope(q_l, cos, sin)
    k_l = apply_axial_rope(k_l, cos, sin)
    k_all = jnp.concatenate([k_l, k_c], axis=3)
    v_all = jnp.concatenate([v_l, v_c], axis=2)

    B_, H, _, S, d = q_l.shape
    nblk = S // Q_BLOCK
    qb = jnp.moveaxis(q_l.reshape(B_, H, 2, nblk, Q_BLOCK, d), 3, 0)
    ob = lax.map(lambda qq: diff_attend(qq, k_all, v_all, lam), qb)
    o_l = jnp.moveaxis(ob, 0, 2).reshape(B_, H, S, ATT_V_DIM)
    y_lat = finish(o_l, g_l)
    y_ctx = None
    if need_ctx_out:
        y_ctx = finish(diff_attend(q_c, k_c, v_c, lam), g_c)
    return y_lat, y_ctx

def first_inputs(seed: int = 0) -> dict:
    key = jax.random.key(seed)
    ks = jax.random.split(key, 24)
    f32 = jnp.float32
    D, W = D_MODEL, LRU_WIDTH
    u = jax.random.uniform(ks[11], (N_LRU, 2, W), f32, 0.9, 0.999)
    a = u ** (1.0 / LRU_C)
    return {
        "x": jax.random.normal(ks[0], (BATCH, SEQ, D), f32),
        "c": jax.random.normal(ks[1], (BATCH, D), f32),
        "ctx": jax.random.normal(ks[2], (BATCH, CTX_LEN, D), f32),
        "c_ctx": jax.random.normal(ks[3], (D,), f32),
        "mod_w": jax.random.normal(ks[4], (DEPTH, D, 3 * D), f32) * (0.5 * D ** -0.5),
        "mod_b": jax.random.normal(ks[5], (DEPTH, 3 * D), f32) * 0.01,
        "norm_g": 1.0 + 0.1 * jax.random.normal(ks[6], (DEPTH, D), f32),
        "lru_w_in": jax.random.normal(ks[7], (N_LRU, D, 2 * W), f32) * D ** -0.5,
        "lru_conv_w": jax.random.normal(ks[8], (N_LRU, CONV_W, W), f32) * CONV_W ** -0.5,
        "lru_conv_b": jax.random.normal(ks[9], (N_LRU, W), f32) * 0.01,
        "lru_gate_w": jax.random.normal(ks[10], (N_LRU, 2, 2, LRU_BLOCKS, LRU_BLOCK, LRU_BLOCK), f32) * LRU_BLOCK ** -0.5,
        "lru_gate_b": jax.random.normal(ks[12], (N_LRU, 2, 2, LRU_BLOCKS, LRU_BLOCK), f32) * 0.01,
        "lru_lambda": jnp.log(a) - jnp.log1p(-a),
        "lru_w_out": jax.random.normal(ks[13], (N_LRU, W, D), f32) * W ** -0.5,
        "att_w_in": jax.random.normal(ks[14], (N_ATT, D, 4 * ATT_WIDTH), f32) * D ** -0.5,
        "att_q_norm": 1.0 + 0.1 * jax.random.normal(ks[15], (N_ATT, ATT_HEAD_DIM), f32),
        "att_k_norm": 1.0 + 0.1 * jax.random.normal(ks[16], (N_ATT, ATT_HEAD_DIM), f32),
        "att_lambda": 0.1 * jax.random.normal(ks[17], (N_ATT, 4, ATT_HEAD_DIM), f32),
        "att_subln": 1.0 + 0.1 * jax.random.normal(ks[18], (N_ATT, ATT_V_DIM), f32),
        "att_w_out": jax.random.normal(ks[19], (N_ATT, ATT_WIDTH, D), f32) * ATT_WIDTH ** -0.5,
    }

def first_block(x, c, ctx, c_ctx, mod_w, mod_b, norm_g, lru_w_in, lru_conv_w, lru_conv_b, lru_gate_w,
              lru_gate_b, lru_lambda, lru_w_out, att_w_in, att_q_norm, att_k_norm, att_lambda,
              att_subln, att_w_out):
    S = x.shape[1]
    cos, sin = axial_rope_tables(S)
    sc = jax.nn.silu(c)
    scc = jax.nn.silu(c_ctx)
    for i in range(DEPTH):
        need_ctx_out = i < DEPTH - 1
        shift, scale, gate = jnp.split(sc @ mod_w[i] + mod_b[i], 3, axis=-1)
        cshift, cscale, cgate = jnp.split(scc @ mod_w[i] + mod_b[i], 3, axis=-1)
        h_lat = rms_norm(x, norm_g[i]) * (1.0 + scale[:, None]) + shift[:, None]
        h_ctx = rms_norm(ctx, norm_g[i]) * (1.0 + cscale) + cshift
        j = i // N_MIXERS
        if i % N_MIXERS == 0:
            y_lat, y_ctx = rglru_mixer(h_lat, h_ctx, lru_w_in[j], lru_conv_w[j], lru_conv_b[j],
                                       lru_gate_w[j], lru_gate_b[j], lru_lambda[j], lru_w_out[j],
                                       need_ctx_out)
        else:
            lam_init = 0.8 - 0.6 * math.exp(-0.3 * i)
            y_lat, y_ctx = diff_attn_mixer(h_lat, h_ctx, att_w_in[j], att_q_norm[j], att_k_norm[j],
                                           att_lambda[j], att_subln[j], att_w_out[j], lam_init,
                                           cos, sin, need_ctx_out)
        x = x + gate[:, None] * y_lat
        if need_ctx_out:
            ctx = ctx + cgate * y_ctx
    return x


D_MIX = D_MODEL
SGU_WIDTH = D_MIX // 2
SGU_GROUPS = 8
SGU_GROUP_DIM = SGU_WIDTH // SGU_GROUPS
CHUNK = 128
ATTN_WIDTH = D_MIX - SGU_WIDTH
HEAD_DIM = 128
N_Q_HEADS = ATTN_WIDTH // HEAD_DIM
N_KV_HEADS = 2
KV_WIDTH = N_KV_HEADS * HEAD_DIM
ROPE_THETA = 10000.0
SPLIT_POINTS = (
    SGU_WIDTH,
    2 * SGU_WIDTH,
    3 * SGU_WIDTH,
    3 * SGU_WIDTH + ATTN_WIDTH,
    3 * SGU_WIDTH + ATTN_WIDTH + KV_WIDTH,
    3 * SGU_WIDTH + ATTN_WIDTH + 2 * KV_WIDTH,
)
KV_START = SPLIT_POINTS[3]
KV_END = SPLIT_POINTS[5]
D_IN = SPLIT_POINTS[5] + ATTN_WIDTH


def rms_norm_2(x, w):
    xf = x.astype(jnp.float32)
    y = xf * lax.rsqrt(jnp.mean(xf * xf, axis=-1, keepdims=True) + EPS)
    return (y * w.astype(jnp.float32)).astype(x.dtype)

def modulation(cond, w_mod, b_mod):
    m = jax.nn.silu(cond) @ w_mod + b_mod
    m = m.reshape(-1, 1, 3 * D_MODEL)
    return jnp.split(m, 3, axis=-1)

def axial_rope_tables_2(n_tokens, dtype):
    rows = n_tokens // GRID_W
    row_id = jnp.broadcast_to(jnp.arange(rows)[:, None], (rows, GRID_W)).reshape(-1)
    col_id = jnp.broadcast_to(jnp.arange(GRID_W)[None, :], (rows, GRID_W)).reshape(-1)
    axis_dim = HEAD_DIM // 2
    inv_freq = ROPE_THETA ** (-jnp.arange(0, axis_dim, 2, dtype=jnp.float32) / axis_dim)
    ang_r = row_id.astype(jnp.float32)[:, None] * inv_freq[None, :]
    ang_c = col_id.astype(jnp.float32)[:, None] * inv_freq[None, :]
    ang = jnp.concatenate([ang_r, ang_r, ang_c, ang_c], axis=-1)
    return jnp.cos(ang).astype(dtype), jnp.sin(ang).astype(dtype)

def _rotate_half(t):
    t1, t2 = jnp.split(t, 2, axis=-1)
    return jnp.concatenate([-t2, t1], axis=-1)

def apply_axial_rope_2(x, cos, sin):
    x_r, x_c = jnp.split(x, 2, axis=-1)
    rot = jnp.concatenate([_rotate_half(x_r), _rotate_half(x_c)], axis=-1)
    return x * cos + rot * sin

def split_heads(t, n_heads):
    b, n, _ = t.shape
    return t.reshape(b, n, n_heads, HEAD_DIM).transpose(0, 2, 1, 3)

def merge_heads(t):
    b, h, n, d = t.shape
    return t.transpose(0, 2, 1, 3).reshape(b, n, h * d)

def kv_heads(k, v, k_norm_w):
    return rms_norm_2(split_heads(k, N_KV_HEADS), k_norm_w), split_heads(v, N_KV_HEADS)

def blocked_gqa(q, k, v):
    b, hq, nq, d = q.shape
    rep = hq // N_KV_HEADS
    qb = q.reshape(b, N_KV_HEADS, rep, nq // Q_BLOCK, Q_BLOCK, d)
    qb = jnp.moveaxis(qb, 3, 0)
    scale = HEAD_DIM ** -0.5

    def one_block(q_blk):
        s = jnp.einsum('bgrqd,bgkd->bgrqk', q_blk, k, preferred_element_type=jnp.float32) * scale
        p = jax.nn.softmax(s, axis=-1).astype(v.dtype)
        return jnp.einsum('bgrqk,bgkd->bgrqd', p, v)

    o = lax.map(one_block, qb)
    return jnp.moveaxis(o, 0, 3).reshape(b, hq, nq, d)

def chunk_sgu(u, v, w_sgu, b_sgu, v_norm_w):
    b, n, _ = u.shape
    u = jax.nn.gelu(u)
    v = jax.nn.gelu(v).reshape(b, n // CHUNK, CHUNK, SGU_GROUPS, SGU_GROUP_DIM)
    v = rms_norm_2(v, v_norm_w)
    s = jnp.einsum('gpq,bcqgd->bcpgd', w_sgu, v) + b_sgu.T[:, :, None]
    return u * s.reshape(b, n, SGU_WIDTH)

def second_inputs(seed: int = 0) -> dict:
    key = jax.random.key(seed)
    ks = jax.random.split(key, 16)
    f32 = jnp.float32
    nrm = lambda k, shape: jax.random.normal(k, shape, f32)
    return {
        "x": nrm(ks[0], (BATCH, SEQ, D_MODEL)),
        "c": nrm(ks[1], (BATCH, D_MODEL)),
        "ctx": nrm(ks[2], (BATCH, CTX_LEN, D_MODEL)),
        "c_ctx": nrm(ks[3], (D_MODEL,)),
        "norm_w": 1.0 + 0.02 * nrm(ks[4], (DEPTH, D_MODEL)),
        "w_mod": 0.5 * D_MODEL ** -0.5 * nrm(ks[5], (DEPTH, D_MODEL, 3 * D_MODEL)),
        "b_mod": 0.01 * nrm(ks[6], (DEPTH, 3 * D_MODEL)),
        "w_in": D_MODEL ** -0.5 * nrm(ks[7], (DEPTH, D_MODEL, D_IN)),
        "w_sgu": CHUNK ** -0.5 * nrm(ks[8], (DEPTH, SGU_GROUPS, CHUNK, CHUNK)),
        "b_sgu": 1.0 + 0.02 * nrm(ks[9], (DEPTH, SGU_GROUPS, CHUNK)),
        "v_norm_w": 1.0 + 0.02 * nrm(ks[10], (DEPTH, SGU_GROUPS, SGU_GROUP_DIM)),
        "q_norm_w": 1.0 + 0.02 * nrm(ks[11], (DEPTH, HEAD_DIM)),
        "k_norm_w": 1.0 + 0.02 * nrm(ks[12], (DEPTH, HEAD_DIM)),
        "w_out": D_MIX ** -0.5 * nrm(ks[13], (DEPTH, D_MIX, D_MODEL)),
    }

def second_block(x, c, ctx, c_ctx, norm_w, w_mod, b_mod, w_in, w_sgu, b_sgu, v_norm_w,
              q_norm_w, k_norm_w, w_out):
    n_lat = x.shape[1]
    cos, sin = axial_rope_tables_2(n_lat, x.dtype)
    xc = ctx
    for layer in range(DEPTH):
        last = layer == DEPTH - 1
        shift, scale, gate = modulation(c, w_mod[layer], b_mod[layer])
        shift_c, scale_c, gate_c = modulation(c_ctx, w_mod[layer], b_mod[layer])
        h = rms_norm_2(x, norm_w[layer]) * (1.0 + scale) + shift
        hc = rms_norm_2(xc, norm_w[layer]) * (1.0 + scale_c) + shift_c

        if last:
            proj_kv_c = hc @ w_in[layer][:, KV_START:KV_END]
            k_c, v_c = jnp.split(proj_kv_c, 2, axis=-1)
            kc, vc = kv_heads(k_c, v_c, k_norm_w[layer])
        else:
            proj_c = hc @ w_in[layer]
            u_c, v_c_sgu, za_c, q_c, k_c, v_c, zb_c = jnp.split(proj_c, SPLIT_POINTS, axis=-1)
            kc, vc = kv_heads(k_c, v_c, k_norm_w[layer])
            qc = rms_norm_2(split_heads(q_c, N_Q_HEADS), q_norm_w[layer])
            attn_c = blocked_gqa(qc, kc, vc)
            sgu_c = chunk_sgu(u_c, v_c_sgu, w_sgu[layer], b_sgu[layer], v_norm_w[layer])
            y_c = jnp.concatenate([sgu_c * jax.nn.silu(za_c),
                                   merge_heads(attn_c) * jax.nn.silu(zb_c)], axis=-1) @ w_out[layer]

        proj = h @ w_in[layer]
        u, v_sgu, za, q, k, v, zb = jnp.split(proj, SPLIT_POINTS, axis=-1)
        q = apply_axial_rope_2(rms_norm_2(split_heads(q, N_Q_HEADS), q_norm_w[layer]), cos, sin)
        k, v = kv_heads(k, v, k_norm_w[layer])
        k = apply_axial_rope_2(k, cos, sin)
        k_all = jnp.concatenate([kc, k], axis=2)
        v_all = jnp.concatenate([vc, v], axis=2)
        attn = blocked_gqa(q, k_all, v_all)
        sgu = chunk_sgu(u, v_sgu, w_sgu[layer], b_sgu[layer], v_norm_w[layer])
        y = jnp.concatenate([sgu * jax.nn.silu(za),
                             merge_heads(attn) * jax.nn.silu(zb)], axis=-1) @ w_out[layer]
        x = x + gate * y
        if not last:
            xc = xc + gate_c * y_c
    return x


def setup_inputs(seed=0):
    out = dict(first_inputs(seed))
    for name, value in second_inputs(seed + 1).items():
        if name != "x":
            out[name + "_2"] = value
    return out


def reference(
    x, c, ctx, c_ctx, mod_w, mod_b, norm_g, lru_w_in, lru_conv_w, lru_conv_b, lru_gate_w,
    lru_gate_b, lru_lambda, lru_w_out, att_w_in, att_q_norm, att_k_norm, att_lambda, att_subln,
    att_w_out, c_2, ctx_2, c_ctx_2, norm_w_2, w_mod_2, b_mod_2, w_in_2, w_sgu_2, b_sgu_2,
    v_norm_w_2, q_norm_w_2, k_norm_w_2, w_out_2,
):
    x = first_block(
        x, c, ctx, c_ctx, mod_w, mod_b, norm_g, lru_w_in, lru_conv_w, lru_conv_b, lru_gate_w,
        lru_gate_b, lru_lambda, lru_w_out, att_w_in, att_q_norm, att_k_norm, att_lambda,
        att_subln, att_w_out,
    )
    return second_block(
        x, c_2, ctx_2, c_ctx_2, norm_w_2, w_mod_2, b_mod_2, w_in_2, w_sgu_2, b_sgu_2,
        v_norm_w_2, q_norm_w_2, k_norm_w_2, w_out_2,
    )


_drawn_inputs = setup_inputs


def setup_inputs(seed=0):
    import zlib

    import numpy as np

    out = dict(_drawn_inputs(seed))
    spreads = {}
    factors = {'lru_conv_b': 2.991,
     'lru_gate_b': 8.0,
     'att_q_norm': 8.0,
     'att_k_norm': 8.0,
     'att_lambda': 8.0,
     'att_subln': 5.278,
     'ctx_2': 6.038,
     'norm_w_2': 8.0,
     'b_mod_2': 7.638,
     'b_sgu_2': 8.0,
     'v_norm_w_2': 8.0,
     'q_norm_w_2': 8.0,
     'k_norm_w_2': 8.0}
    for name, (base, spread) in spreads.items():
        noise = np.random.default_rng([zlib.crc32(name.encode()), seed]).standard_normal(out[name].shape)
        drawn = base * np.exp(spread * noise) if base else spread * noise
        out[name] = __import__('jax').numpy.asarray(drawn.astype(out[name].dtype))
    for name, factor in factors.items():
        out[name] = (out[name] * factor).astype(out[name].dtype)
    return out
```

```python
from contextlib import ExitStack
import math

import numpy as np
import concourse.bass as bass
from concourse import mybir

F32 = mybir.dt.float32
F32R = mybir.dt.float32r
ALU = mybir.AluOpType
ACT = mybir.ActivationFunctionType
AX_X = mybir.AxisListType.X

P = 128
D = 2048
KT = D // P
T = 256
NT = 2 * T
TT = T // P
EPS = 1e-6
HALF = KT // 2

BLOCKS = 16
HEADS1 = 16
HD1 = 64
LAM_INIT = 0.8 - 0.6 * math.exp(-0.3)
GROUPS = 8
HEADS2 = 8
KV2 = 2
REP2 = HEADS2 // KV2
SCALE2 = float(P) ** -0.5

S_LRU = 0
S_LRU_OUT = S_LRU + 2 * BLOCKS
S_ATT = S_LRU_OUT + KT
S_ATT_OUT = S_ATT + 4 * HEADS1
S_NET2 = S_ATT_OUT + KT
L2_KV = 3 * GROUPS
L2_ATT = L2_KV + 2 * KV2
L2_OUT = L2_ATT + 2 * HEADS2
L2_STRIPS = L2_OUT + KT
N_STRIPS = S_NET2 + 2 * L2_STRIPS

MOD_GROUPS = 48
MOD_FIRST = 8
M_LRU = MOD_FIRST
M_ATT = M_LRU + BLOCKS
M_SGU = M_ATT + HEADS1

_widths = dict(c=4 * KT, norm_g=4 * KT, mod_b=4 * 48, conv_w=4 * BLOCKS, conv_b=BLOCKS, gate_b=4 * BLOCKS,
               lam=2 * BLOCKS, v_norm=2 * GROUPS, qk2=4, qk1=2, subln=1, att_lam=4)
COL, _at = {}, 0
for _n, _w in _widths.items():
    COL[_n] = (_at, _at + _w)
    _at += _w
N_COLS = _at


def build(nc, ins, out):
    with ExitStack() as ctx:
        def sb(name, shape, dt=F32):
            return ctx.enter_context(nc.sbuf_tensor(name, shape, dt))

        def sems(phase, names):
            return {n: ctx.enter_context(nc.semaphore(phase + n)) for n in names.split()}

        xl = sb("xl", [P, KT, T])
        y = sb("y", [P, 2, KT, T])
        h_hi = sb("h_hi", [P, KT, NT], F32R)
        h_lo = sb("h_lo", [P, KT, NT], F32R)
        raw = sb("raw", [P, 4, HALF * P])
        w_hi = sb("w_hi", [P, 2, 2, HALF * P], F32R)
        w_lo = sb("w_lo", [P, 2, 2, HALF * P], F32R)
        modraw = sb("modraw", [P, 2, 4, 512])
        mod = sb("mod", [P, 192, 2])
        cols = sb("cols", [P, N_COLS])
        cond = sb("cond", [P, KT, 32])
        consts = sb("consts", [P, 5 * P + 4 + 4 * T])
        small = sb("small", [P, 256])
        modrow = sb("modrow", [P, 512])
        WORK = 4288
        work = sb("work", [P, WORK])
        psum = ctx.enter_context(nc.psum_tensor("psum", [P, 8, 512], F32))

        ident, ones = consts[:, 0:P], consts[:, P:2 * P]
        ones64, rot1, rot2 = (consts[:, n * P:(n + 1) * P] for n in (2, 3, 4))
        sel = [consts[:, 5 * P + 2 * n:5 * P + 2 * n + 2] for n in range(2)]
        tab = 5 * P + 4
        cos1, sin1, cos2, sin2 = (consts[:, tab + n * T:tab + (n + 1) * T] for n in range(4))

        def col(name, a, n=1):
            return cols[:, bass.ds(COL[name][0] + a, n)]

        class Space:

            def __init__(self, *parts):
                self.parts = [[p, n, 0] for p, n in parts]

            def __call__(self, n):
                for part in self.parts:
                    if part[2] + n <= part[1]:
                        part[2] += n
                        return part[0][:, part[2] - n:part[2]]
                raise ValueError("work space")

        work_all = (work, WORK)
        xl_all = (xl[:, :, :].rearrange("p k t -> p (k t)"), KT * T)
        yc_all = (y[:, 1, :, :].rearrange("p k t -> p (k t)"), KT * T)
        modraw_all = (modraw[:, :, :, :].rearrange("p a b c -> p (a b c)"), 4096)

        def two(ap):
            return ap.rearrange("p (s t) -> p s t", s=2)

        _small_at = [0]

        def tiny(n):
            _small_at[0] += n
            assert _small_at[0] <= 256
            return small[:, _small_at[0] - n:_small_at[0]]

        neg_sp4, sp4 = tiny(2 * BLOCKS), tiny(2 * BLOCKS)
        half_gb = tiny(4 * BLOCKS)
        qg1, subg, lam_col = tiny(1), tiny(1), tiny(1)
        mod_a = tiny(2 * KT).rearrange("p (k s) -> p k s", s=2)
        eps_col = tiny(1)

        S = sems("", 
            "consts_in cols_in x_in ctx2_in raw_in0 raw_in1 raw_in2 raw_in3 split_hi split_lo strip_done "
            "modraw_in0 modraw_in1 mod_used modrow_ready modcol_ps mod_cols "
            "pads_zero cond_tanh cond_ready start_dve start_act start_pe start_tab "
            "sq_done sq_added ss_done sd_done rstd_done t_done hf_done hhi_done h_ready "
            "y_hi y_ready res_in0 res_in1 x_new out_stored "
        )
        raw_in = [S["raw_in0"], S["raw_in1"], S["raw_in2"], S["raw_in3"]]
        modraw_in = [S["modraw_in0"], S["modraw_in1"]]
        res_in = [S["res_in0"], S["res_in1"]]
        L = sems("lru_", "gw_in0 gw_in1 u_evac conv_step xc_ready tg_done silu_done gate_done gates_tanh coef_step "
                 "coef_done m_done sqrt_done bx_done b_done scan_done ysum_done lru_y")
        gw_in = [L["gw_in0"], L["gw_in1"]]
        A = sems("att_", "k_evac q_evac v_evac tg sgl ssk ssq sso sdk sdq sdo rsk rsq rso kn qn rotk rotq kt1 kr qt1 qr "
                 "scores smax negmax expd rsum rlam p1s attn attn_t attn_sb v_t v_sb av o_evac on att_y")
        G = sems("sgu_", "tab_in0 tab_in1 gu gv tz sz v_t sqv ssv sdv rsv vn s sb1 sb2 gu_y")
        B = sems("gqa_", "k_evac v_evac ssk sdk rsk kn rotk kt1 kr v_t v_sb "
                 "q_evac tz sz ssq sdq rsq qn rotq qt1 qr scores smax negmax expd rsum attn attn_t attn_sb av y2")

        def ge(eng, sem, value):
            if not (isinstance(value, int) and value <= 0):
                eng.wait_ge(sem, value)

        class Chain:

            def __init__(self, eng, sem, done, per):
                self.eng, self.sem, self.done, self.per, self.n = eng, sem, done, per, 0

            def __call__(self, ins):
                self.n += 1
                ins.then_inc(self.sem, 1)
                self.eng.wait_ge(self.sem, self.done + self.n)

            def close(self):
                assert self.n == self.per, (self.n, self.per)

        class Strip:

            def __init__(self, base, c, j=0, per=2):
                assert base % 2 == 0 and per % 2 == 0
                self.pair, self.par = (base + c) // 2 + (per // 2) * j, c % 2
                self.s = 2 * self.pair + self.par

        def load_strip(sp, pair, par, first=False):
            s = 2 * pair + par
            for half in range(2):
                if not first:
                    sp.wait_ge(S["split_lo"], 2 * (s - 2) + half + 1)
                sp.dma_start(raw[:, 2 * par + half, :], ins["weights"][2 * s + half]).then_inc(raw_in[2 * par + half], 16)

        def split_hi(act, pair, par):
            s = 2 * pair + par
            for half in range(2):
                act.wait_ge(raw_in[2 * par + half], 16 * (pair + 1))
                if half == 0:
                    ge(act, S["strip_done"], s - 1)
                act.activation(w_hi[:, par, half, :], raw[:, 2 * par + half, :], ACT.Copy).then_inc(S["split_hi"], 1)

        def split_lo(dve, pair, par):
            s = 2 * pair + par
            for half in range(2):
                dve.wait_ge(S["split_hi"], 2 * s + half + 1)
                if half == 0:
                    ge(dve, S["strip_done"], s - 1)
                dve.tensor_tensor(w_lo[:, par, half, :], raw[:, 2 * par + half, :],
                                  w_hi[:, par, half, :].bitcast(F32), ALU.subtract).then_inc(S["split_lo"], 1)

        def next_strip(split, eng, st):
            if not (isinstance(st.pair, int) and 2 * st.pair + st.par + 2 >= N_STRIPS):
                split(eng, st.pair + 1, st.par)

        def strip(pe, st, dst, n, between=None, operand=None):
            for half in range(2):
                pe.wait_ge(S["split_lo"], 2 * st.s + half + 1)
                for kk in range(HALF):
                    k = half * HALF + kk
                    if operand is not None:
                        pe.wait_ge(operand[0], operand[1] + k + 1)
                    hi, lo = (w[:, st.par, half, kk * P:(kk + 1) * P] for w in (w_hi, w_lo))
                    pe.matmul(dst, hi, h_hi[:, k, 0:n], start=(k == 0), stop=False)
                    pe.matmul(dst, hi, h_lo[:, k, 0:n], start=False, stop=False)
                    mm = pe.matmul(dst, lo, h_hi[:, k, 0:n], start=False, stop=(k == KT - 1))
                if half == 1:
                    mm.then_inc(S["strip_done"], 1)
                if between is not None:
                    between(half)

        pmod = psum[:, 7, :]

        def mod_load(pool, m, q, first=False):
            if not first:
                pool.wait_ge(S["mod_used"], 4 * m + q - 1)
            pool.dma_start(modraw[:, q % 2, :, :], ins["mod_weights"][4 * m + q]).then_inc(modraw_in[q % 2], 16)

        def mod_chunk(pe, m, q):
            pe.wait_ge(modraw_in[q % 2], 16 * (2 * m + q // 2 + 1))
            if q == 0:
                ge(pe, S["mod_cols"], m)
            for j in range(4):
                mm = pe.matmul(pmod[32 * j:32 * j + 32, :], cond[:, 4 * q + j, :], modraw[:, q % 2, j, :],
                               start=(q == 0), stop=(q == 3))
            mm.then_inc(S["mod_used"], 1)

        def mod_rows(act, m):
            act.wait_ge(S["mod_used"], 4 * m + 4)
            ge(act, S["modcol_ps"], m)
            act.activation(modrow[:, :], pmod, ACT.Copy).then_inc(S["modrow_ready"], 1)

        def mod_turn(pe, m, net):
            pe.wait_ge(S["modrow_ready"], m + 1)
            for b in range(4):
                mm = pe.matmul(pmod[:, 2 * b:2 * b + 2], modrow[:, b * P:(b + 1) * P], sel[net], start=True, stop=True)
            mm.then_inc(S["modcol_ps"], 1)

        def mod_add(dve, m):
            dve.wait_ge(S["modcol_ps"], m + 1)
            dve.tensor_tensor(mod[:, bass.ds(4 * m, 4), :], pmod[:, 0:8].rearrange("p (b s) -> p b s", s=2),
                              col("mod_b", 4 * m, 4).unsqueeze(2).to_broadcast([P, 4, 2]), ALU.add).then_inc(S["mod_cols"], 1)

        def normalize_bufs(space):
            return dict(rstd=space(NT), t=[space(NT) for _ in range(2)], hf=[space(NT) for _ in range(2)])

        w0 = Space(work_all)
        acc = w0(NT)
        sqb = [w0(NT), w0(NT)]
        res = [w0(NT), w0(NT)]
        nb = normalize_bufs(Space((work[:, NT:WORK], WORK - NT)))
        SS_BANK = 6

        def norm_pe(pe, l):
            pe.wait_ge(S["sq_added"], 16 * (l + 1))
            pe.matmul(psum[:, SS_BANK, :], ones, acc, start=True, stop=True).then_inc(S["ss_done"], 1)

        def norm_act(act, l):
            act.wait_ge(S["ss_done"], l + 1)
            act.activation(nb["rstd"], psum[:, SS_BANK, :], ACT.Sqrt, scale=1.0 / D, bias=eps_col).then_inc(S["sd_done"], 1)
            if l > 0:
                act.wait_ge(S["strip_done"], layer_strip[l])

            def tile(k, par):
                act.wait_ge(S["hf_done"], KT * l + k + 1)
                act.activation(h_hi[:, k, :], nb["hf"][par], ACT.Copy).then_inc(S["hhi_done"], 1)
            with act.Fori(0, KT // 2) as j:
                for par in range(2):
                    tile(2 * j + par, par)

        def norm_pool(pool, l):
            pool.wait_ge(S["rstd_done"], l + 1)

            def tile(k, par, first):
                if not first:
                    pool.wait_ge(S["hf_done"], KT * l + k - 1)
                pool.tensor_tensor(nb["t"][par][:, 0:T], xl[:, k, :], nb["rstd"][:, 0:T], ALU.mult)
                pool.tensor_tensor(nb["t"][par][:, T:NT], y[:, 1, k, :], nb["rstd"][:, T:NT], ALU.mult).then_inc(S["t_done"], 1)
            for par in range(2):
                tile(par, par, True)
            with pool.Fori(1, KT // 2) as j:
                for par in range(2):
                    tile(2 * j + par, par, False)

        def norm_dve(dve, l):
            dve.wait_ge(S["mod_cols"], 12 * l + 8)
            dve.wait_ge(S["sd_done"], l + 1)
            dve.scalar_tensor_tensor(
                out=mod_a, in0=mod[:, 48 * l + 16:48 * l + 32, :], scalar=1.0,
                in1=col("norm_g", KT * l, KT).unsqueeze(2).to_broadcast([P, KT, 2]), op0=ALU.add, op1=ALU.mult)
            dve.reciprocal(nb["rstd"], nb["rstd"]).then_inc(S["rstd_done"], 1)
            dve.wait_ge(S["rstd_done"], l + 1)
            if l > 0:
                dve.wait_ge(S["strip_done"], layer_strip[l])

            def high(k, par, first):
                dve.wait_ge(S["t_done"], KT * l + k + 1)
                if not first:
                    dve.wait_ge(S["h_ready"], KT * l + k - 1)
                for s in range(2):
                    ins_ = dve.tensor_scalar(nb["hf"][par][:, s * T:(s + 1) * T], nb["t"][par][:, s * T:(s + 1) * T],
                                             mod_a[:, bass.ds(k, 1), s], mod[:, bass.ds(48 * l + k, 1), s],
                                             ALU.mult, ALU.add)
                ins_.then_inc(S["hf_done"], 1)

            def low(k, par):
                dve.wait_ge(S["hhi_done"], KT * l + k + 1)
                dve.tensor_tensor(h_lo[:, k, :], nb["hf"][par], h_hi[:, k, :].bitcast(F32), ALU.subtract).then_inc(S["h_ready"], 1)
            high(0, 0, True)
            high(1, 1, True)
            low(0, 0)
            with dve.Fori(1, KT // 2) as j:
                high(2 * j, 0, False)
                low(2 * j - 1, 1)
                high(2 * j + 1, 1, False)
                low(2 * j, 0)
            low(KT - 1, 1)

        layer_strip = [S_LRU, S_ATT, S_NET2, S_NET2 + L2_STRIPS]
        out_strip = [S_LRU_OUT, S_ATT_OUT, S_NET2 + L2_OUT, S_NET2 + L2_STRIPS + L2_OUT]
        wide = [True, False, True, False]
        n_of = [NT if w else T for w in wide]
        fetched = [0, 2]
        y_sem = [L["lru_y"], A["att_y"], B["y2"], B["y2"]]
        y_count = [BLOCKS, HEADS1, HEADS2, 2 * HEADS2]

        def y_view(l, k):
            return y[:, :, k, :] if wide[l] else y[:, 0, k, :]

        def h_view(h, l, k):
            return two(h[:, k, :]) if wide[l] else h[:, k, 0:T]

        def out_pe(pe, l):
            n = n_of[l]
            for c in range(2):
                st = Strip(out_strip[l], c)
                strip(pe, st, psum[:, c, 0:n], n, operand=(S["y_ready"], KT * l) if c == 0 else None)
            with pe.Fori(1, KT // 2) as j:
                for c in range(2):
                    st = Strip(out_strip[l], c, j)
                    pe.wait_ge(S["x_new"], KT * l + 2 * j + c - 1)
                    strip(pe, st, psum[:, c, 0:n], n)

        def out_act(act, l):
            n = n_of[l]
            act.wait_ge(y_sem[l], y_count[l])
            act.wait_ge(S["strip_done"], out_strip[l])
            with act.Fori(0, KT) as k:
                act.activation(h_view(h_hi, l, k), y_view(l, k), ACT.Copy).then_inc(S["y_hi"], 1)

            def tile(j, c, last):
                st = Strip(out_strip[l], c, j)
                act.wait_ge(S["strip_done"], st.s + 1)
                if not last:
                    next_strip(split_hi, act, st)
                if l < 3:
                    m = 2 * j + c
                    act.wait_ge(S["x_new"], KT * l + m + 1)
                    if not (isinstance(j, int) and j == 0):
                        act.wait_ge(S["sq_added"], sq_base[l + 1] + m - 1)
                    act.activation(sqb[c][:, 0:T], xl[:, m, :], ACT.Square)
                    if wide[l]:
                        ins_ = act.activation(sqb[c][:, T:NT], y[:, 1, m, :], ACT.Square)
                    else:
                        act.wait_ge(S["ctx2_in"], 16)
                        ins_ = act.activation(sqb[c][:, T:NT], y[:, 1, m, :], ACT.Square)
                    ins_.then_inc(S["sq_done"], 1)
            for c in range(2):
                tile(0, c, False)
            with act.Fori(1, KT // 2 - 1) as j:
                for c in range(2):
                    tile(j, c, False)
            for c in range(2):
                tile(KT // 2 - 1, c, l == 3)

        sq_base = [0, 16, 32, 48]

        def out_pool(pool, l):
            def fetch(m, c, first):
                if not first:
                    pool.wait_ge(S["x_new"], KT * l + m - 1)
                if l == 0:
                    pool.dma_start(res[c], ins["x_t"][m]).then_inc(res_in[c], 16)
                else:
                    pool.dma_start(res[c][:, T:NT], ins["ctx2_t"][m]).then_inc(res_in[c], 16)

            def add(m, c, first):
                pool.wait_ge(S["sq_done"], sq_base[l + 1] + m + 1)
                if first:
                    pool.tensor_copy(acc, sqb[c]).then_inc(S["sq_added"], 1)
                else:
                    pool.wait_ge(S["sq_added"], sq_base[l + 1] + m)
                    pool.tensor_tensor(acc, acc, sqb[c], ALU.add).then_inc(S["sq_added"], 1)
            if l in fetched:
                pool.wait_ge(y_sem[l], y_count[l])
                for c in range(2):
                    fetch(c, c, True)
            if l < 3:
                for c in range(2):
                    add(c, c, c == 0)
                    if l in fetched:
                        fetch(2 + c, c, False)
                with pool.Fori(1, KT // 2 - 1) as j:
                    for c in range(2):
                        add(2 * j + c, c, False)
                        if l in fetched:
                            fetch(2 * j + 2 + c, c, False)
                for c in range(2):
                    add(KT - 2 + c, c, False)

        def out_dve(dve, l):
            n = n_of[l]
            nth = fetched.index(l) if l in fetched else 0
            with dve.Fori(0, KT) as k:
                dve.wait_ge(S["y_hi"], KT * l + k + 1)
                dve.tensor_tensor(h_view(h_lo, l, k), y_view(l, k), h_view(h_hi, l, k).bitcast(F32),
                                  ALU.subtract).then_inc(S["y_ready"], 1)
            dve.wait_ge(S["mod_cols"], 12 * l + 12)
            dve.wait_ge(S["y_ready"], KT * (l + 1))

            def tile(j, c, last):
                st = Strip(out_strip[l], c, j)
                m = 2 * j + c
                dve.wait_ge(S["strip_done"], st.s + 1)
                if l in fetched:
                    dve.wait_ge(res_in[c], 16 * (KT // 2 * nth + j + 1))
                gate = lambda s: mod[:, bass.ds(48 * l + 32 + m, 1), s]
                if wide[l]:
                    dve.scalar_tensor_tensor(out=y[:, 1, m, :], in0=psum[:, c, T:NT], scalar=gate(1),
                                             in1=res[c][:, T:NT], op0=ALU.mult, op1=ALU.add)
                dve.scalar_tensor_tensor(out=xl[:, m, :], in0=psum[:, c, 0:T], scalar=gate(0),
                                         in1=res[c][:, 0:T] if l == 0 else xl[:, m, :],
                                         op0=ALU.mult, op1=ALU.add).then_inc(S["x_new"], 1)
                if not last:
                    next_strip(split_lo, dve, st)
            with dve.Fori(0, KT // 2 - 1) as j:
                for c in range(2):
                    tile(j, c, False)
            for c in range(2):
                tile(KT // 2 - 1, c, l == 3)

        lsp = Space(xl_all, work_all)
        upad = lsp(2 * 260).rearrange("p (s t) -> p s t", s=2)
        lw = dict(
            tr=[lsp(NT), lsp(NT)], ti=[lsp(NT), lsp(NT)], a=[lsp(NT), lsp(NT)], th=[lsp(NT), lsp(NT)],
            xc=lsp(NT), sg=lsp(NT), gw=[lsp(4 * P).rearrange("p (g d) -> p g d", g=4) for _ in range(2)])
        U_BANK, G_BANK, GATE_BANK = 0, 1, 2
        CONV_W = 4

        def lru_pool(pool):
            def block(b, par, first):
                if not first:
                    pool.wait_ge(L["gate_done"], 4 * (b - 1))
                pool.dma_start(lw["gw"][par], ins["gate_w"][b].rearrange("p (g d) -> p g d", g=4)).then_inc(gw_in[par], 16)
                for q in range(4):
                    mod_load(pool, M_LRU + b, q)
            pool.wait_ge(S["hf_done"], KT)
            pool.wait_ge(S["h_ready"], KT)
            for b in range(2):
                block(b, b, True)
            with pool.Fori(1, BLOCKS // 2) as j:
                for par in range(2):
                    block(2 * j + par, par, False)

        def lru_pe(pe):
            def block(j, par, first):
                b = 2 * j + par
                su, sg = Strip(S_LRU, 2 * par, j, 4), Strip(S_LRU, 2 * par + 1, j, 4)
                ge(pe, L["u_evac"], b)
                strip(pe, su, psum[:, U_BANK, :], NT, between=lambda half: mod_chunk(pe, M_LRU + b, half),
                      operand=(S["h_ready"], 0) if first else None)
                ge(pe, L["silu_done"], b)
                strip(pe, sg, psum[:, G_BANK, :], NT, between=lambda half: mod_chunk(pe, M_LRU + b, 2 + half))
                pe.wait_ge(L["xc_ready"], b + 1)
                pe.wait_ge(gw_in[par], 16 * (j + 1))
                for g in range(4):
                    ge(pe, L["gates_tanh"], 4 * (b - 1) + g + 1)
                    pe.matmul(psum[:, GATE_BANK + g, :], lw["gw"][par][:, g, :], lw["xc"], start=True, stop=True).then_inc(L["gate_done"], 1)
                mod_turn(pe, M_LRU + b, 0)
            block(0, 0, True)
            block(0, 1, False)
            with pe.Fori(1, BLOCKS // 2) as j:
                for par in range(2):
                    block(j, par, False)

        def lru_act(act):
            def block(j, par):
                b = 2 * j + par
                su, sg = Strip(S_LRU, 2 * par, j, 4), Strip(S_LRU, 2 * par + 1, j, 4)
                act.wait_ge(S["strip_done"], su.s + 1)
                ge(act, L["xc_ready"], b)
                act.activation(upad[:, :, 2:2 + T], two(psum[:, U_BANK, :]), ACT.Copy).then_inc(L["u_evac"], 1)
                next_strip(split_hi, act, su)
                act.wait_ge(S["strip_done"], sg.s + 1)
                ge(act, L["lru_y"], b)
                act.activation(lw["sg"], psum[:, G_BANK, :], ACT.Tanh, scale=0.5).then_inc(L["tg_done"], 1)
                next_strip(split_hi, act, sg)
                mod_rows(act, M_LRU + b)
                ge(act, L["scan_done"], 4 * b)
                for d in range(2):
                    for g, dst in enumerate((lw["tr"][d], lw["ti"][d])):
                        act.wait_ge(L["gate_done"], 4 * b + 2 * d + g + 1)
                        act.activation(dst, psum[:, GATE_BANK + 2 * d + g, :], ACT.Tanh, scale=0.5,
                                       bias=half_gb[:, bass.ds(4 * b + 2 * d + g, 1)]).then_inc(L["gates_tanh"], 1)
                act.wait_ge(L["gates_tanh"], 4 * b + 4)
                for d in range(2):
                    act.activation(lw["a"][d], lw["tr"][d], ACT.Exp, scale=neg_sp4[:, bass.ds(2 * b + d, 1)],
                                   bias=neg_sp4[:, bass.ds(2 * b + d, 1)])
                    act.activation(lw["th"][d], lw["tr"][d], ACT.Tanh, scale=sp4[:, bass.ds(2 * b + d, 1)],
                                   bias=sp4[:, bass.ds(2 * b + d, 1)]).then_inc(L["coef_step"], 1)
                for d in range(2):
                    act.wait_ge(L["coef_step"], 2 * b + d + 1)
                    act.activation(lw["tr"][d], lw["a"][d], ACT.Square).then_inc(L["coef_done"], 1)
                for d in range(2):
                    act.wait_ge(L["m_done"], 2 * b + d + 1)
                    act.activation(lw["th"][d], lw["th"][d], ACT.Sqrt, scale=0.25).then_inc(L["sqrt_done"], 1)
            block(0, 0)
            block(0, 1)
            with act.Fori(1, BLOCKS // 2) as j:
                for par in range(2):
                    block(j, par)

        def lru_dve(dve):
            dve.memset(upad[:, :, 0:2], 0.0)
            dve.memset(upad[:, :, 2 + T:], 0.0).then_inc(S["pads_zero"], 1)
            dve.wait_ge(S["pads_zero"], 1)

            def block(j, par):
                b = 2 * j + par
                su, sg = Strip(S_LRU, 2 * par, j, 4), Strip(S_LRU, 2 * par + 1, j, 4)
                dve.wait_ge(L["u_evac"], b + 1)
                if not (isinstance(b, int) and b == 0):
                    dve.wait_ge(L["gate_done"], 4 * b)
                xc = two(lw["xc"])
                step = Chain(dve, L["conv_step"], 3 * b, 3)
                step(dve.tensor_scalar(xc, upad[:, :, 0:T], col("conv_w", 4 * b), col("conv_b", b), ALU.mult, ALU.add))
                for w in range(1, CONV_W):
                    ins_ = dve.scalar_tensor_tensor(out=xc, in0=upad[:, :, w:w + T], scalar=col("conv_w", 4 * b + w),
                                                    in1=xc, op0=ALU.mult, op1=ALU.add)
                    if w < CONV_W - 1:
                        step(ins_)
                ins_.then_inc(L["xc_ready"], 1)
                step.close()
                next_strip(split_lo, dve, su)
                dve.wait_ge(L["tg_done"], b + 1)
                dve.scalar_tensor_tensor(out=lw["sg"], in0=lw["sg"], scalar=1.0, in1=psum[:, G_BANK, :],
                                         op0=ALU.add, op1=ALU.mult).then_inc(L["silu_done"], 1)
                next_strip(split_lo, dve, sg)
                mod_add(dve, M_LRU + b)
                for d in range(2):
                    dve.wait_ge(L["coef_done"], 2 * b + d + 1)
                    dve.scalar_tensor_tensor(out=lw["th"][d], in0=lw["tr"][d], scalar=1.0, in1=lw["th"][d],
                                             op0=ALU.add, op1=ALU.mult).then_inc(L["m_done"], 1)
                dve.wait_ge(L["xc_ready"], b + 1)
                for d in range(2):
                    dve.scalar_tensor_tensor(out=lw["ti"][d], in0=lw["ti"][d], scalar=1.0, in1=lw["xc"],
                                             op0=ALU.add, op1=ALU.mult).then_inc(L["bx_done"], 1)
                for d in range(2):
                    dve.wait_ge(L["sqrt_done"], 2 * b + d + 1)
                    dve.wait_ge(L["bx_done"], 2 * b + d + 1)
                    dve.tensor_tensor(lw["ti"][d], lw["ti"][d], lw["th"][d], ALU.mult).then_inc(L["b_done"], 1)
                dve.wait_ge(L["m_done"], 2 * b + 2)
                hs = lw["tr"]
                for d, (a, bb) in enumerate(((slice(T, NT), NT - 1), (slice(NT - 1, T - 1, -1), T))):
                    dve.wait_ge(L["b_done"], 2 * b + d + 1)
                    dve.tensor_tensor_scan(hs[d][:, a], lw["a"][d][:, a], lw["ti"][d][:, a], 0.0, ALU.mult, ALU.add).then_inc(L["scan_done"], 1)
                for d, (a, bb) in enumerate(((slice(0, T), NT - 1), (slice(T - 1, None, -1), T))):
                    dve.wait_ge(L["scan_done"], 4 * b + d + 1)
                    dve.tensor_tensor_scan(hs[d][:, a], lw["a"][d][:, a], lw["ti"][d][:, a], hs[d][:, bb:bb + 1],
                                           ALU.mult, ALU.add).then_inc(L["scan_done"], 1)
                dve.wait_ge(L["scan_done"], 4 * b + 4)
                dve.tensor_tensor(lw["a"][0], hs[0], hs[1], ALU.add).then_inc(L["ysum_done"], 1)
                dve.wait_ge(L["ysum_done"], b + 1)
                dve.wait_ge(L["silu_done"], b + 1)
                dve.scalar_tensor_tensor(out=y[:, :, b, :], in0=two(lw["a"][0]), scalar=0.5, in1=two(lw["sg"]),
                                         op0=ALU.mult, op1=ALU.mult).then_inc(L["lru_y"], 1)
            block(0, 0)
            block(0, 1)
            with dve.Fori(1, BLOCKS // 2) as j:
                for par in range(2):
                    block(j, par)


        def rounds(eng, body, n, lag, peel=2):
            for i in range(peel):
                body(i // 2, i % 2)
            with eng.Fori(peel // 2, n // 2) as j:
                for par in range(2):
                    body(j, par)
            for i in range(n, n + lag):
                body(i // 2, i % 2)

        def live(i, n):
            return not isinstance(i, int) or 0 <= i < n

        asp = Space(yc_all, work_all)
        ksb, ksq, kr, vt_sb, v_sb = (asp(NT) for _ in range(5))
        p1 = [[asp(NT) for _ in range(2)] for _ in range(2)]
        attn1_t = asp(4 * T).rearrange("p (k q) -> p k q", k=4)
        qsb, qsq, qr, rtmp, osb, osq = (asp(T) for _ in range(6))
        sg1 = [asp(T), asp(T)]
        mx1, nm1, rs1 = tiny(4), tiny(4), tiny(4)
        K_BANK, Q_BANK, S_BANK, R_BANK, V_BANK, O_BANK, M_BANK = 0, 1, 2, 4, 4, 5, 6

        def att_strip(j, par, c):
            return Strip(S_ATT, 4 * par + c, j, 8)

        def att_pool(pool):
            with pool.Fori(0, HEADS1) as i:
                for q in range(4):
                    mod_load(pool, M_ATT + i, q)

        def att_pe(pe):
            def body(j, par):
                i = 2 * j + par
                here, before, older = live(i, HEADS1), live(i - 1, HEADS1), live(i - 2, HEADS1)

                def chunk(q):
                    return lambda half: mod_chunk(pe, M_ATT + i, q) if half else None
                first = isinstance(i, int) and i == 0
                if here:
                    ge(pe, A["v_evac"], i)
                    strip(pe, att_strip(j, par, 0), psum[:, K_BANK, :], NT, chunk(0),
                          operand=(S["h_ready"], KT) if first else None)
                if before:
                    pe.wait_ge(A["qr"], i)
                    pe.wait_ge(A["kr"], i)
                    ge(pe, A["attn_sb"], 2 * (i - 1))
                    pe.wait_ge(A["v_sb"], i)
                    ge(pe, A["o_evac"], i - 1)
                    for qt in range(2):
                        for c in range(2):
                            rows = slice(HD1 * c, HD1 * c + HD1)
                            mm = pe.matmul(psum[:, S_BANK + 2 * qt + c, :], qr[rows, qt * P:(qt + 1) * P], kr[rows, :],
                                           start=True, stop=True)
                        mm.then_inc(A["scores"], 1)
                if older:
                    pe.wait_ge(A["o_evac"], i - 1)
                    pe.matmul(psum[:, M_BANK, 0:T], ones, osq, start=True, stop=True).then_inc(A["sso"], 1)
                if here:
                    ge(pe, A["sgl"], i)
                    strip(pe, att_strip(j, par, 1), psum[:, Q_BANK, 0:T], T, chunk(1))
                    pe.wait_ge(A["k_evac"], i + 1)
                    if older:
                        pe.wait_ge(A["sdo"], i - 1)
                    if before:
                        pe.wait_ge(A["qr"], i)
                    pe.matmul(psum[:, M_BANK, :], ones64, ksq, start=True, stop=True).then_inc(A["ssk"], 1)
                    strip(pe, att_strip(j, par, 2), psum[:, K_BANK, :], NT, chunk(2))
                    pe.wait_ge(A["q_evac"], i + 1)
                    pe.wait_ge(A["sdk"], i + 1)
                    pe.matmul(psum[:, M_BANK, 0:T], ones64, qsq, start=True, stop=True).then_inc(A["ssq"], 1)
                    pe.wait_ge(A["kn"], i + 1)
                    ge(pe, A["expd"], 4 * i)
                    pe.matmul(psum[:, R_BANK, 0:T], rot1, ksb[:, 0:T], start=True, stop=True).then_inc(A["rotk"], 1)
                if before:
                    for qt in range(2):
                        pe.wait_ge(A["attn"], 2 * (i - 1) + qt + 1)
                        for kt in range(4):
                            mm = pe.transpose(psum[:, S_BANK + qt, kt * P:(kt + 1) * P], p1[qt][0][:, kt * P:(kt + 1) * P], ident)
                        mm.then_inc(A["attn_t"], 1)
                if here:
                    strip(pe, att_strip(j, par, 3), psum[:, Q_BANK, 0:T], T, chunk(3))
                    pe.wait_ge(A["qn"], i + 1)
                    pe.wait_ge(A["sdq"], i + 1)
                    pe.matmul(psum[:, M_BANK, 0:T], rot1, qsb, start=True, stop=True).then_inc(A["rotq"], 1)
                if before:
                    pe.wait_ge(A["attn_sb"], 2 * i)
                    pe.wait_ge(A["v_sb"], i)
                    for kt in range(4):
                        mm = pe.matmul(psum[:, O_BANK, 0:T], v_sb[:, kt * P:(kt + 1) * P], attn1_t[:, kt, :],
                                       start=(kt == 0), stop=(kt == 3))
                    mm.then_inc(A["av"], 1)
                if here:
                    pe.wait_ge(A["v_evac"], i + 1)
                    pe.wait_ge(A["kt1"], i + 1)
                    for t in range(4):
                        mm = pe.transpose(psum[:, V_BANK, t * P:(t + 1) * P], vt_sb[:, t * P:(t + 1) * P], ident)
                    mm.then_inc(A["v_t"], 1)
                    mod_turn(pe, M_ATT + i, 1)
            rounds(pe, body, HEADS1, 2)

        def att_act(act):
            def body(j, par):
                i = 2 * j + par
                here, before, older = live(i, HEADS1), live(i - 1, HEADS1), live(i - 2, HEADS1)
                if here:
                    st = att_strip(j, par, 0)
                    act.wait_ge(S["strip_done"], st.s + 1)
                    ge(act, A["kr"], i)
                    act.activation(ksb, psum[:, K_BANK, :], ACT.Copy)
                    act.activation(ksq, psum[:, K_BANK, :], ACT.Square).then_inc(A["k_evac"], 1)
                    next_strip(split_hi, act, st)
                if before:
                    ge(act, A["attn_t"], 2 * (i - 1))
                    for qt in range(2):
                        act.wait_ge(A["negmax"], 2 * (i - 1) + qt + 1)
                        for c in range(2):
                            n = 2 * qt + c
                            act.activation(p1[qt][c], psum[:, S_BANK + n, :], ACT.Exp, bias=nm1[:, n:n + 1],
                                           accum_out=rs1[:, n:n + 1]).then_inc(A["expd"], 1)
                if older:
                    act.wait_ge(A["sso"], i - 1)
                    act.activation(osq, psum[:, M_BANK, 0:T], ACT.Sqrt, scale=1.0 / P, bias=eps_col).then_inc(A["sdo"], 1)
                if here:
                    st = att_strip(j, par, 1)
                    act.wait_ge(S["strip_done"], st.s + 1)
                    ge(act, A["qr"], i)
                    act.activation(qsb, psum[:, Q_BANK, 0:T], ACT.Copy)
                    act.activation(qsq, psum[:, Q_BANK, 0:T], ACT.Square).then_inc(A["q_evac"], 1)
                    next_strip(split_hi, act, st)
                    act.wait_ge(A["ssk"], i + 1)
                    act.activation(ksq, psum[:, M_BANK, :], ACT.Sqrt, scale=1.0 / HD1, bias=eps_col).then_inc(A["sdk"], 1)
                    st = att_strip(j, par, 2)
                    act.wait_ge(S["strip_done"], st.s + 1)
                    ge(act, A["v_t"], i)
                    act.activation(vt_sb, psum[:, K_BANK, :], ACT.Copy).then_inc(A["v_evac"], 1)
                    next_strip(split_hi, act, st)
                    act.wait_ge(A["ssq"], i + 1)
                    act.activation(qsq, psum[:, M_BANK, 0:T], ACT.Sqrt, scale=1.0 / HD1, bias=eps_col).then_inc(A["sdq"], 1)
                if before:
                    ge(act, A["av"], i - 1)
                    for qt in range(2):
                        act.wait_ge(A["attn_t"], 2 * (i - 1) + qt + 1)
                        act.activation(attn1_t[:, :, qt * P:(qt + 1) * P],
                                       psum[:, S_BANK + qt, :].rearrange("p (k q) -> p k q", k=4), ACT.Copy).then_inc(A["attn_sb"], 1)
                if here:
                    st = att_strip(j, par, 3)
                    act.wait_ge(S["strip_done"], st.s + 1)
                    ge(act, A["att_y"], i - 1)
                    act.activation(sg1[par], psum[:, Q_BANK, 0:T], ACT.Tanh, scale=0.5).then_inc(A["tg"], 1)
                    next_strip(split_hi, act, st)
                    mod_rows(act, M_ATT + i)
                if before:
                    act.wait_ge(A["av"], i)
                    ge(act, A["att_y"], i - 1)
                    act.activation(osb, psum[:, O_BANK, 0:T], ACT.Copy)
                    act.activation(osq, psum[:, O_BANK, 0:T], ACT.Square).then_inc(A["o_evac"], 1)
                if here:
                    act.wait_ge(A["v_t"], i + 1)
                    ge(act, A["av"], i)
                    act.activation(v_sb, psum[:, V_BANK, :], ACT.Copy).then_inc(A["v_sb"], 1)
            rounds(act, body, HEADS1, 2)

        def att_dve(dve):
            kg = col("qk1", 1)

            def body(j, par):
                i = 2 * j + par
                here, before, older = live(i, HEADS1), live(i - 1, HEADS1), live(i - 2, HEADS1)
                if here:
                    next_strip(split_lo, dve, att_strip(j, par, 0))
                if before:
                    for qt in range(2):
                        two_c = slice(2 * qt, 2 * qt + 2)
                        dve.wait_ge(A["scores"], 2 * (i - 1) + qt + 1)
                        dve.tensor_reduce(mx1[:, two_c], psum[:, S_BANK + 2 * qt:S_BANK + 2 * qt + 2, :], AX_X, ALU.max).then_inc(A["smax"], 1)
                        dve.wait_ge(A["smax"], 2 * (i - 1) + qt + 1)
                        dve.tensor_scalar(nm1[:, two_c], mx1[:, two_c], -1.0, None, ALU.mult).then_inc(A["negmax"], 1)
                if older:
                    dve.wait_ge(A["sdo"], i - 1)
                    dve.reciprocal(osq, osq).then_inc(A["rso"], 1)
                    dve.wait_ge(A["rso"], i - 1)
                    dve.scalar_tensor_tensor(out=osb, in0=osb, scalar=subg, in1=osq, op0=ALU.mult, op1=ALU.mult).then_inc(A["on"], 1)
                    dve.wait_ge(A["on"], i - 1)
                    dve.tensor_tensor(y[:, 0, i - 2, :], osb, sg1[par], ALU.mult).then_inc(A["att_y"], 1)
                if before:
                    for qt in range(2):
                        dve.wait_ge(A["expd"], 4 * (i - 1) + 2 * qt + 2)
                        dve.reciprocal(rs1[:, 2 * qt:2 * qt + 2], rs1[:, 2 * qt:2 * qt + 2]).then_inc(A["rsum"], 1)
                        dve.wait_ge(A["rsum"], 2 * (i - 1) + qt + 1)
                        dve.tensor_scalar(p1[qt][1], p1[qt][1], rs1[:, 2 * qt + 1:2 * qt + 2], lam_col, ALU.mult, ALU.mult).then_inc(A["p1s"], 1)
                        dve.wait_ge(A["p1s"], 2 * (i - 1) + qt + 1)
                        dve.scalar_tensor_tensor(out=p1[qt][0], in0=p1[qt][0], scalar=rs1[:, 2 * qt:2 * qt + 1], in1=p1[qt][1],
                                                 op0=ALU.mult, op1=ALU.subtract).then_inc(A["attn"], 1)
                if here:
                    next_strip(split_lo, dve, att_strip(j, par, 1))
                    dve.wait_ge(A["sdk"], i + 1)
                    dve.reciprocal(ksq, ksq).then_inc(A["rsk"], 1)
                    dve.wait_ge(A["rsk"], i + 1)
                    dve.scalar_tensor_tensor(out=kr[:, T:NT], in0=ksb[:, T:NT], scalar=kg, in1=ksq[:, T:NT], op0=ALU.mult, op1=ALU.mult)
                    dve.scalar_tensor_tensor(out=ksb[:, 0:T], in0=ksb[:, 0:T], scalar=kg, in1=ksq[:, 0:T], op0=ALU.mult, op1=ALU.mult).then_inc(A["kn"], 1)
                    next_strip(split_lo, dve, att_strip(j, par, 2))
                    dve.wait_ge(A["kn"], i + 1)
                    dve.tensor_tensor(kr[:, 0:T], ksb[:, 0:T], cos1, ALU.mult)
                    dve.wait_ge(A["rotk"], i + 1)
                    if before:
                        dve.wait_ge(A["qr"], i)
                    dve.tensor_tensor(rtmp, psum[:, R_BANK, 0:T], sin1, ALU.mult).then_inc(A["kt1"], 1)
                    dve.wait_ge(A["kt1"], i + 1)
                    dve.tensor_tensor(kr[:, 0:T], kr[:, 0:T], rtmp, ALU.add).then_inc(A["kr"], 1)
                    dve.wait_ge(A["sdq"], i + 1)
                    dve.reciprocal(qsq, qsq).then_inc(A["rsq"], 1)
                    dve.wait_ge(A["rsq"], i + 1)
                    dve.scalar_tensor_tensor(out=qsb, in0=qsb, scalar=qg1, in1=qsq, op0=ALU.mult, op1=ALU.mult).then_inc(A["qn"], 1)
                    next_strip(split_lo, dve, att_strip(j, par, 3))
                    dve.wait_ge(A["tg"], i + 1)
                    dve.scalar_tensor_tensor(out=sg1[par], in0=sg1[par], scalar=1.0, in1=psum[:, Q_BANK, 0:T],
                                             op0=ALU.add, op1=ALU.mult).then_inc(A["sgl"], 1)
                    dve.wait_ge(A["qn"], i + 1)
                    dve.wait_ge(A["kr"], i + 1)
                    dve.tensor_tensor(qr, qsb, cos1, ALU.mult)
                    dve.wait_ge(A["rotq"], i + 1)
                    dve.tensor_tensor(rtmp, psum[:, M_BANK, 0:T], sin1, ALU.mult).then_inc(A["qt1"], 1)
                    dve.wait_ge(A["qt1"], i + 1)
                    dve.tensor_tensor(qr, qr, rtmp, ALU.add).then_inc(A["qr"], 1)
                    mod_add(dve, M_ATT + i)
            rounds(dve, body, HEADS1, 2)

        gsp = Space(work_all)
        gu = [gsp(NT), gsp(NT)]
        gv, sz2, sqv, vn, gtmp = (gsp(NT) for _ in range(5))
        tabs = [gsp(2 * P), gsp(2 * P)]
        ssv = tiny(4)
        GU_BANK, GV_BANK, GZ_BANK, GT_BANK, GS_BANK = range(5)

        def sgu_strip(lay, j, par, c):
            return Strip(S_NET2 + lay * L2_STRIPS, 3 * par + c, j, 6)

        def sgu_pool(pool, lay):
            base = GROUPS * lay
            mods = lay == 0

            def table(g, par, first):
                if not first:
                    pool.wait_ge(G["gu_y"], base + g - 1)
                pool.dma_start(tabs[par], ins["sgu_tab"][base + g]).then_inc([G["tab_in0"], G["tab_in1"]][par], 16)
            pool.wait_ge(S["h_ready"], KT * (3 + lay))
            for par in range(2):
                table(par, par, True)
            def mod_group(g):
                if mods:
                    for q in range(4):
                        mod_load(pool, M_SGU + g, q)
            mod_group(0)
            with pool.Fori(0, GROUPS // 2 - 1) as j:
                for par in range(2):
                    mod_group(2 * j + par + 1)
                    table(2 * j + 2 + par, par, False)
            mod_group(GROUPS - 1)

        def sgu_pe(pe, lay):
            base, n, mods = GROUPS * lay, NT if lay == 0 else T, lay == 0
            nt = n // P

            def body(j, par):
                i = 2 * j + par
                here, before = live(i, GROUPS), live(i - 1, GROUPS)

                def chunk(q):
                    return lambda half: mod_chunk(pe, M_SGU + i, q) if half and mods else None
                if here:
                    ge(pe, G["gu"], base + i)
                    strip(pe, sgu_strip(lay, j, par, 0), psum[:, GU_BANK, 0:n], n, chunk(0),
                          operand=(S["h_ready"], KT * (2 + lay)) if isinstance(i, int) and i == 0 else None)
                if before:
                    pe.wait_ge(G["vn"], base + i)
                    tab = tabs[1 - par]
                    pe.wait_ge([G["tab_in0"], G["tab_in1"]][1 - par], 16 * (base // 2 + (j if par else j - 1) + 1))
                    ge(pe, G["sb1"], base + i - 1)
                    for t in range(nt):
                        mm = pe.matmul(psum[:, GS_BANK, t * P:(t + 1) * P], vn[:, t * P:(t + 1) * P], tab[:, 0:P],
                                       start=True, stop=True)
                    mm.then_inc(G["s"], 1)
                if here:
                    ge(pe, G["gv"], base + i)
                    strip(pe, sgu_strip(lay, j, par, 1), psum[:, GV_BANK, 0:n], n, chunk(1))
                    ge(pe, G["sz"], base + i)
                    strip(pe, sgu_strip(lay, j, par, 2), psum[:, GZ_BANK, 0:n], n, chunk(2))
                    pe.wait_ge(G["gv"], base + i + 1)
                    ge(pe, G["vn"], base + i)
                    for t in range(nt):
                        mm = pe.transpose(psum[:, GT_BANK, t * P:(t + 1) * P], gv[:, t * P:(t + 1) * P], ident)
                    mm.then_inc(G["v_t"], 1)
                    if mods:
                        mod_chunk(pe, M_SGU + i, 3)
                        mod_turn(pe, M_SGU + i, 1)
            rounds(pe, body, GROUPS, 1)

        def sgu_act(act, lay):
            base, n, mods = GROUPS * lay, NT if lay == 0 else T, lay == 0
            nt = n // P

            def body(j, par):
                i = 2 * j + par
                if not live(i, GROUPS):
                    return
                st = sgu_strip(lay, j, par, 0)
                act.wait_ge(S["strip_done"], st.s + 1)
                ge(act, G["gu_y"], base + i - 1)
                act.activation(gu[par][:, 0:n], psum[:, GU_BANK, 0:n], ACT.Gelu_apprx_tanh).then_inc(G["gu"], 1)
                next_strip(split_hi, act, st)
                st = sgu_strip(lay, j, par, 1)
                act.wait_ge(S["strip_done"], st.s + 1)
                ge(act, G["v_t"], base + i)
                act.activation(gv[:, 0:n], psum[:, GV_BANK, 0:n], ACT.Gelu_apprx_tanh).then_inc(G["gv"], 1)
                next_strip(split_hi, act, st)
                st = sgu_strip(lay, j, par, 2)
                act.wait_ge(S["strip_done"], st.s + 1)
                ge(act, G["gu_y"], base + i)
                act.activation(sz2[:, 0:n], psum[:, GZ_BANK, 0:n], ACT.Tanh, scale=0.5).then_inc(G["tz"], 1)
                next_strip(split_hi, act, st)
                act.wait_ge(G["v_t"], base + i + 1)
                ge(act, G["ssv"], base + i)
                act.activation(sqv[:, 0:n], psum[:, GT_BANK, 0:n], ACT.Square).then_inc(G["sqv"], 1)
                if mods:
                    mod_rows(act, M_SGU + i)
                act.wait_ge(G["ssv"], base + i + 1)
                act.activation(ssv[:, 0:nt], ssv[:, 0:nt], ACT.Sqrt, scale=1.0 / P, bias=eps_col).then_inc(G["sdv"], 1)
            rounds(act, body, GROUPS, 1)

        def sgu_dve(dve, lay):
            base, n, mods = GROUPS * lay, NT if lay == 0 else T, lay == 0
            nt = n // P

            def tiles(ap):
                return ap[:, 0:n].rearrange("p (t d) -> p t d", d=P)

            def body(j, par):
                i = 2 * j + par
                here, before = live(i, GROUPS), live(i - 1, GROUPS)
                if here:
                    next_strip(split_lo, dve, sgu_strip(lay, j, par, 0))
                if before:
                    tab = tabs[1 - par]
                    dve.wait_ge(G["s"], base + i)
                    dve.scalar_tensor_tensor(out=tiles(gtmp), in0=tiles(psum[:, GS_BANK, :]), scalar=col("v_norm", base + i - 1),
                                             in1=tab[:, P:2 * P].unsqueeze(1).to_broadcast([P, nt, P]),
                                             op0=ALU.mult, op1=ALU.add).then_inc(G["sb1"], 1)
                    dve.wait_ge(G["sb1"], base + i)
                    dve.tensor_tensor(gtmp[:, 0:n], gtmp[:, 0:n], gu[1 - par][:, 0:n], ALU.mult).then_inc(G["sb2"], 1)
                    dve.wait_ge(G["sb2"], base + i)
                    if lay == 0:
                        dve.scalar_tensor_tensor(out=y[:, :, i - 1, :], in0=two(gtmp), scalar=0.5, in1=two(sz2),
                                                 op0=ALU.mult, op1=ALU.mult).then_inc(G["gu_y"], 1)
                    else:
                        dve.scalar_tensor_tensor(out=y[:, 0, i - 1, :], in0=gtmp[:, 0:n], scalar=0.5, in1=sz2[:, 0:n],
                                                 op0=ALU.mult, op1=ALU.mult).then_inc(G["gu_y"], 1)
                if here:
                    next_strip(split_lo, dve, sgu_strip(lay, j, par, 1))
                    dve.wait_ge(G["tz"], base + i + 1)
                    dve.scalar_tensor_tensor(out=sz2[:, 0:n], in0=sz2[:, 0:n], scalar=1.0, in1=psum[:, GZ_BANK, 0:n],
                                             op0=ALU.add, op1=ALU.mult).then_inc(G["sz"], 1)
                    next_strip(split_lo, dve, sgu_strip(lay, j, par, 2))
                    dve.wait_ge(G["sqv"], base + i + 1)
                    dve.tensor_reduce(ssv[:, 0:nt], tiles(sqv), AX_X, ALU.add).then_inc(G["ssv"], 1)
                    if mods:
                        mod_add(dve, M_SGU + i)
                    dve.wait_ge(G["sdv"], base + i + 1)
                    dve.reciprocal(ssv[:, 0:nt], ssv[:, 0:nt]).then_inc(G["rsv"], 1)
                    dve.wait_ge(G["rsv"], base + i + 1)
                    ge(dve, G["s"], base + i)
                    for t in range(nt):
                        ins_ = dve.tensor_scalar(vn[:, t * P:(t + 1) * P], psum[:, GT_BANK, t * P:(t + 1) * P], ssv[:, t:t + 1],
                                                 None, ALU.mult)
                    ins_.then_inc(G["vn"], 1)
            rounds(dve, body, GROUPS, 1)

        bsp = Space(modraw_all, work_all)
        k2 = [bsp(NT), bsp(NT)]
        v2 = [bsp(NT), bsp(NT)]
        q2, q2s, q2r = (bsp(NT) for _ in range(3))
        r2tmp = bsp(T)
        p2 = [bsp(NT), bsp(NT), bsp(NT)]
        at2 = bsp(4 * T).rearrange("p (k q) -> p k q", k=4)
        at2c = bsp(2 * T).rearrange("p (k q) -> p k q", k=2)
        sz3 = [bsp(NT), bsp(NT)]
        mx2, nm2, rs2 = tiny(4), tiny(4), tiny(4)
        kv_k, kv_sq, kv_v = p2[0:2], p2[2], [q2, q2r]

        def kv_strip(lay, c):
            return Strip(S_NET2 + lay * L2_STRIPS + L2_KV, c)

        def kv_pe(pe, lay):
            base = 2 * lay
            pe.wait_ge(G["gu_y"], GROUPS * (lay + 1))
            if lay == 0:
                pe.wait_ge(S["mod_cols"], MOD_GROUPS)
            for n in range(2):
                strip(pe, kv_strip(lay, n), psum[:, n, :], NT)
            for n in range(2):
                pe.wait_ge(B["k_evac"], base + n + 1)
                if n:
                    pe.wait_ge(B["sdk"], base + n)
                pe.matmul(psum[:, 6, :], ones, kv_sq, start=True, stop=True).then_inc(B["ssk"], 1)
                strip(pe, kv_strip(lay, 2 + n), psum[:, n, :], NT)
                pe.wait_ge(B["kn"], base + n + 1)
                if n:
                    pe.wait_ge(B["kt1"], base + n)
                pe.matmul(psum[:, 5, 0:T], rot2, kv_k[n][:, 0:T], start=True, stop=True).then_inc(B["rotk"], 1)
            for n in range(2):
                pe.wait_ge(B["v_evac"], base + n + 1)
                for t in range(4):
                    mm = pe.transpose(psum[:, 3 + n, t * P:(t + 1) * P], kv_v[n][:, t * P:(t + 1) * P], ident)
                mm.then_inc(B["v_t"], 1)

        def kv_act(act, lay):
            base = 2 * lay
            act.wait_ge(G["gu_y"], GROUPS * (lay + 1))
            for n in range(2):
                st = kv_strip(lay, n)
                act.wait_ge(S["strip_done"], st.s + 1)
                act.activation(kv_k[n], psum[:, n, :], ACT.Copy)
                if n:
                    act.wait_ge(B["kn"], base + n)
                act.activation(kv_sq, psum[:, n, :], ACT.Square).then_inc(B["k_evac"], 1)
                next_strip(split_hi, act, st)
                act.wait_ge(B["ssk"], base + n + 1)
                act.activation(kv_sq, psum[:, 6, :], ACT.Sqrt, scale=1.0 / P, bias=eps_col).then_inc(B["sdk"], 1)
            for n in range(2):
                st = kv_strip(lay, 2 + n)
                act.wait_ge(S["strip_done"], st.s + 1)
                act.activation(kv_v[n], psum[:, n, :], ACT.Copy).then_inc(B["v_evac"], 1)
                next_strip(split_hi, act, st)
            for n in range(2):
                act.wait_ge(B["v_t"], base + n + 1)
                act.activation(v2[n], psum[:, 3 + n, :], ACT.Copy).then_inc(B["v_sb"], 1)

        def kv_dve(dve, lay):
            base = 2 * lay
            kg = col("qk2", 2 + lay)
            for n in range(2):
                next_strip(split_lo, dve, kv_strip(lay, n))
                dve.wait_ge(B["sdk"], base + n + 1)
                dve.reciprocal(kv_sq, kv_sq).then_inc(B["rsk"], 1)
                dve.wait_ge(B["rsk"], base + n + 1)
                dve.scalar_tensor_tensor(out=k2[n][:, T:NT], in0=kv_k[n][:, T:NT], scalar=kg, in1=kv_sq[:, T:NT], op0=ALU.mult, op1=ALU.mult)
                dve.scalar_tensor_tensor(out=kv_k[n][:, 0:T], in0=kv_k[n][:, 0:T], scalar=kg, in1=kv_sq[:, 0:T],
                                         op0=ALU.mult, op1=ALU.mult).then_inc(B["kn"], 1)
            for n in range(2):
                next_strip(split_lo, dve, kv_strip(lay, 2 + n))
                dve.wait_ge(B["kn"], base + n + 1)
                dve.tensor_tensor(k2[n][:, 0:T], kv_k[n][:, 0:T], cos2, ALU.mult)
                dve.wait_ge(B["rotk"], base + n + 1)
                if n:
                    dve.wait_ge(B["kr"], base + n)
                dve.tensor_tensor(r2tmp, psum[:, 5, 0:T], sin2, ALU.mult).then_inc(B["kt1"], 1)
                dve.wait_ge(B["kt1"], base + n + 1)
                dve.tensor_tensor(k2[n][:, 0:T], k2[n][:, 0:T], r2tmp, ALU.add).then_inc(B["kr"], 1)

        def gqa_strip(lay, j, par, c):
            return Strip(S_NET2 + lay * L2_STRIPS + L2_ATT, 2 * par + c, j, 4)

        def gqa_pe(pe, lay):
            base, wide_ = HEADS2 * lay, lay == 0
            n = NT if wide_ else T
            pe.wait_ge(B["kr"], 2 * (lay + 1))
            pe.wait_ge(B["v_sb"], 2 * (lay + 1))

            def body(j, par):
                i = 2 * j + par
                here, before, older = live(i, HEADS2), live(i - 1, HEADS2), live(i - 2, HEADS2)
                if here:
                    ge(pe, B["q_evac"], base + i)
                    strip(pe, gqa_strip(lay, j, par, 0), psum[:, 0, 0:n], n)
                if before:
                    pe.wait_ge(B["qn"], base + i)
                    ge(pe, B["qt1"], base + i - 1)
                    pe.matmul(psum[:, 5, 0:T], rot2, q2[:, 0:T], start=True, stop=True).then_inc(B["rotq"], 1)
                if older:
                    pe.wait_ge(B["attn"], base + i - 1)
                    for qt in range(2):
                        for kt in range(4):
                            mm = pe.transpose(psum[:, 2 + qt, kt * P:(kt + 1) * P], p2[qt][:, kt * P:(kt + 1) * P], ident)
                    if wide_:
                        for qt in range(2):
                            for kt in range(2):
                                mm = pe.transpose(psum[:, 4, kt * T + qt * P:kt * T + (qt + 1) * P],
                                                  p2[2][:, qt * T + kt * P:qt * T + (kt + 1) * P], ident)
                    mm.then_inc(B["attn_t"], 1)
                if here:
                    ge(pe, B["sz"], base + i)
                    strip(pe, gqa_strip(lay, j, par, 1), psum[:, 1, 0:n], n)
                    pe.wait_ge(B["q_evac"], base + i + 1)
                    ge(pe, B["sdq"], base + i)
                    pe.matmul(psum[:, 6, 0:n], ones, q2s[:, 0:n], start=True, stop=True).then_inc(B["ssq"], 1)
                if older:
                    pe.wait_ge(B["attn_sb"], base + i - 1)
                    ge(pe, B["y2"], base + i - 2)
                    for kt in range(4):
                        mm = pe.matmul(psum[:, 7, 0:T], v2[par][:, kt * P:(kt + 1) * P], at2[:, kt, :], start=(kt == 0), stop=(kt == 3))
                    if wide_:
                        for kt in range(2):
                            mm = pe.matmul(psum[:, 7, T:NT], v2[par][:, T + kt * P:T + (kt + 1) * P], at2c[:, kt, :],
                                           start=(kt == 0), stop=(kt == 1))
                    mm.then_inc(B["av"], 1)
                if before:
                    pe.wait_ge(B["qr"], base + i)
                    ge(pe, B["attn_sb"], base + i - 1)
                    keys = k2[1 - par]
                    for qt in range(2):
                        mm = pe.matmul(psum[:, 2 + qt, :], q2r[:, qt * P:(qt + 1) * P], keys, start=True, stop=True)
                    if wide_:
                        for qt in range(2):
                            mm = pe.matmul(psum[:, 4, qt * T:(qt + 1) * T], q2r[:, T + qt * P:T + (qt + 1) * P], keys[:, T:NT],
                                           start=True, stop=True)
                    mm.then_inc(B["scores"], 1)
            rounds(pe, body, HEADS2, 2, 4)

        def gqa_act(act, lay):
            base, wide_ = HEADS2 * lay, lay == 0
            n = NT if wide_ else T

            def body(j, par):
                i = 2 * j + par
                here, before, older = live(i, HEADS2), live(i - 1, HEADS2), live(i - 2, HEADS2)
                if before:
                    act.wait_ge(B["ssq"], base + i)
                    act.activation(q2s[:, 0:n], psum[:, 6, 0:n], ACT.Sqrt, scale=1.0 / P, bias=eps_col).then_inc(B["sdq"], 1)
                if older:
                    act.wait_ge(B["negmax"], base + i - 1)
                    ge(act, B["attn_t"], base + i - 2)
                    for qt in range(2):
                        ins_ = act.activation(p2[qt], psum[:, 2 + qt, :], ACT.Exp, scale=SCALE2, bias=nm2[:, qt:qt + 1],
                                              accum_out=rs2[:, qt:qt + 1])
                    if wide_:
                        for qt in range(2):
                            ins_ = act.activation(p2[2][:, qt * T:(qt + 1) * T], psum[:, 4, qt * T:(qt + 1) * T], ACT.Exp, scale=SCALE2,
                                                  bias=nm2[:, 2 + qt:3 + qt], accum_out=rs2[:, 2 + qt:3 + qt])
                    ins_.then_inc(B["expd"], 1)
                if here:
                    st = gqa_strip(lay, j, par, 0)
                    act.wait_ge(S["strip_done"], st.s + 1)
                    next_strip(split_hi, act, st)
                    ge(act, B["qr"], base + i)
                    if isinstance(i, int) and i == 0:
                        act.wait_ge(B["v_t"], 2 * (lay + 1))
                    act.activation(q2[:, 0:n], psum[:, 0, 0:n], ACT.Copy)
                    act.activation(q2s[:, 0:n], psum[:, 0, 0:n], ACT.Square).then_inc(B["q_evac"], 1)
                if older:
                    act.wait_ge(B["attn_t"], base + i - 1)
                    ge(act, B["av"], base + i - 2)
                    for qt in range(2):
                        ins_ = act.activation(at2[:, :, qt * P:(qt + 1) * P],
                                              psum[:, 2 + qt, :].rearrange("p (k q) -> p k q", k=4), ACT.Copy)
                    if wide_:
                        ins_ = act.activation(at2c, psum[:, 4, :].rearrange("p (k q) -> p k q", k=2), ACT.Copy)
                    ins_.then_inc(B["attn_sb"], 1)
                if here:
                    st = gqa_strip(lay, j, par, 1)
                    act.wait_ge(S["strip_done"], st.s + 1)
                    next_strip(split_hi, act, st)
                    ge(act, B["y2"], base + i - 1)
                    act.activation(sz3[par][:, 0:n], psum[:, 1, 0:n], ACT.Tanh, scale=0.5).then_inc(B["tz"], 1)
            rounds(act, body, HEADS2, 2, 4)

        def gqa_dve(dve, lay):
            base, wide_ = HEADS2 * lay, lay == 0
            n = NT if wide_ else T
            nq = 4 if wide_ else 2
            qg = col("qk2", lay)

            def body(j, par):
                i = 2 * j + par
                here, before, older = live(i, HEADS2), live(i - 1, HEADS2), live(i - 2, HEADS2)
                if older:
                    dve.wait_ge(B["scores"], base + i - 1)
                    ins_ = dve.tensor_reduce(mx2[:, 0:2], psum[:, 2:4, :], AX_X, ALU.max)
                    if wide_:
                        ins_ = dve.tensor_reduce(mx2[:, 2:4], two(psum[:, 4, :]), AX_X, ALU.max)
                    ins_.then_inc(B["smax"], 1)
                    dve.wait_ge(B["smax"], base + i - 1)
                    dve.tensor_scalar(nm2[:, 0:nq], mx2[:, 0:nq], -SCALE2, None, ALU.mult).then_inc(B["negmax"], 1)
                if before:
                    dve.wait_ge(B["sdq"], base + i)
                    dve.reciprocal(q2s[:, 0:n], q2s[:, 0:n]).then_inc(B["rsq"], 1)
                    dve.wait_ge(B["rsq"], base + i)
                    ge(dve, B["scores"], base + i - 1)
                    if isinstance(i, int) and i == 1:
                        dve.wait_ge(B["v_t"], 2 * (lay + 1))
                    if wide_:
                        dve.scalar_tensor_tensor(out=q2r[:, T:NT], in0=q2[:, T:NT], scalar=qg, in1=q2s[:, T:NT], op0=ALU.mult, op1=ALU.mult)
                    dve.scalar_tensor_tensor(out=q2[:, 0:T], in0=q2[:, 0:T], scalar=qg, in1=q2s[:, 0:T], op0=ALU.mult, op1=ALU.mult).then_inc(B["qn"], 1)
                if older:
                    dve.wait_ge(B["expd"], base + i - 1)
                    dve.reciprocal(rs2[:, 0:nq], rs2[:, 0:nq]).then_inc(B["rsum"], 1)
                    dve.wait_ge(B["rsum"], base + i - 1)
                    for qt in range(2):
                        ins_ = dve.tensor_scalar(p2[qt], p2[qt], rs2[:, qt:qt + 1], None, ALU.mult)
                    if wide_:
                        for qt in range(2):
                            ins_ = dve.tensor_scalar(p2[2][:, qt * T:(qt + 1) * T], p2[2][:, qt * T:(qt + 1) * T], rs2[:, 2 + qt:3 + qt],
                                                     None, ALU.mult)
                    ins_.then_inc(B["attn"], 1)
                if here:
                    next_strip(split_lo, dve, gqa_strip(lay, j, par, 0))
                if before:
                    dve.wait_ge(B["qn"], base + i)
                    dve.tensor_tensor(q2r[:, 0:T], q2[:, 0:T], cos2, ALU.mult)
                    dve.wait_ge(B["rotq"], base + i)
                    ge(dve, B["qr"], base + i - 1)
                    dve.tensor_tensor(r2tmp, psum[:, 5, 0:T], sin2, ALU.mult).then_inc(B["qt1"], 1)
                    dve.wait_ge(B["qt1"], base + i)
                    dve.tensor_tensor(q2r[:, 0:T], q2r[:, 0:T], r2tmp, ALU.add).then_inc(B["qr"], 1)
                if here:
                    next_strip(split_lo, dve, gqa_strip(lay, j, par, 1))
                if older:
                    dve.wait_ge(B["av"], base + i - 1)
                    tile = GROUPS + REP2 * par + (j - 1)
                    if wide_:
                        dve.scalar_tensor_tensor(out=y[:, :, tile, :], in0=two(psum[:, 7, :]), scalar=0.5, in1=two(sz3[par]),
                                                 op0=ALU.mult, op1=ALU.mult).then_inc(B["y2"], 1)
                    else:
                        dve.scalar_tensor_tensor(out=y[:, 0, tile, :], in0=psum[:, 7, 0:T], scalar=0.5, in1=sz3[par][:, 0:T],
                                                 op0=ALU.mult, op1=ALU.mult).then_inc(B["y2"], 1)
                if here:
                    dve.wait_ge(B["tz"], base + i + 1)
                    dve.scalar_tensor_tensor(out=sz3[par][:, 0:n], in0=sz3[par][:, 0:n], scalar=1.0, in1=psum[:, 1, 0:n],
                                             op0=ALU.add, op1=ALU.mult).then_inc(B["sz"], 1)
            rounds(dve, body, HEADS2, 2)

        zt = Space((work[:, 6 * NT:WORK], WORK - 6 * NT))
        ctan = zt(4 * KT)
        sp_n, sp_z, sp_w, sp_r = (zt(2 * BLOCKS) for _ in range(4))
        lam_p, lam_e = zt(2), zt(2)
        LOG1P = [1.0 / (2 * n + 1) for n in range(8, 0, -1)]

        def start_pool(pool):
            pool.memset(cond[:, :, :], 0.0).then_inc(S["start_tab"], 1)
            pool.memset(eps_col, EPS).then_inc(S["start_tab"], 1)

            def add(k, par):
                pool.wait_ge(S["sq_done"], k + 1)
                pool.wait_ge(S["sq_added"], k)
                pool.tensor_tensor(acc, acc, sqb[par], ALU.add).then_inc(S["sq_added"], 1)
            pool.wait_ge(S["sq_done"], 1)
            pool.tensor_copy(acc, sqb[0]).then_inc(S["sq_added"], 1)
            add(1, 1)
            with pool.Fori(1, KT // 2) as j:
                for par in range(2):
                    add(2 * j + par, par)

        def start_act(act):
            act.wait_ge(S["cols_in"], 16)
            act.activation(ctan, col("c", 0, 4 * KT), ACT.Tanh, scale=0.5).then_inc(S["cond_tanh"], 1)
            act.wait_ge(S["start_dve"], 1)
            act.activation(sp_z, sp_z, ACT.Exp, scale=-1.0).then_inc(S["start_act"], 1)
            act.wait_ge(S["start_pe"], 1)
            act.activation(lam_e, psum[:, 0, 0:2], ACT.Exp).then_inc(S["start_act"], 1)
            act.wait_ge(S["x_in"], 32)

            def square(k, par, first):
                if not first:
                    act.wait_ge(S["sq_added"], k - 1)
                act.activation(sqb[par][:, 0:T], xl[:, k, :], ACT.Square)
                act.activation(sqb[par][:, T:NT], y[:, 1, k, :], ACT.Square).then_inc(S["sq_done"], 1)
            for par in range(2):
                square(par, par, True)
            with act.Fori(1, KT // 2) as j:
                for par in range(2):
                    square(2 * j + par, par, False)
            act.wait_ge(S["start_tab"], 2)
            with act.Fori(1, MOD_FIRST) as m:
                act.wait_ge(S["mod_used"], 4 * m)
                act.activation(modrow[:, :], pmod, ACT.Copy).then_inc(S["modrow_ready"], 1)
                act.wait_ge(S["modcol_ps"], m)
            mod_rows(act, MOD_FIRST - 1)

        def start_dve(dve):
            n = [0]

            def step(ins_):
                n[0] += 1
                ins_.then_inc(S["start_dve"], 1)
                dve.wait_ge(S["start_dve"], n[0])
            dve.wait_ge(S["cols_in"], 16)
            lam = col("lam", 0, 2 * BLOCKS)
            dve.scalar_tensor_tensor(out=sp_z, in0=lam, scalar=-1.0, in1=lam, op0=ALU.mult, op1=ALU.max)
            dve.tensor_tensor(lam_p[:, 0:1], col("att_lam", 0), col("att_lam", 1), ALU.mult)
            dve.tensor_scalar(half_gb, col("gate_b", 0, 4 * BLOCKS), 0.5, None, ALU.mult)
            dve.tensor_scalar(qg1, col("qk1", 0), float(HD1) ** -0.5, None, ALU.mult)
            dve.tensor_scalar(subg, col("subln", 0), (1.0 - LAM_INIT) * 0.5, None, ALU.mult)
            dve.tensor_scalar(sp_n, lam, -1.0, 0.0, ALU.mult, ALU.max)
            step(dve.tensor_tensor(lam_p[:, 1:2], col("att_lam", 2), col("att_lam", 3), ALU.mult))
            dve.wait_ge(S["cond_tanh"], 1)
            step(dve.scalar_tensor_tensor(out=ctan, in0=ctan, scalar=1.0, in1=col("c", 0, 4 * KT), op0=ALU.add, op1=ALU.mult))
            dve.wait_ge(S["start_tab"], 1)
            dve.tensor_scalar(cond[:, :, 0:4].rearrange("p k v -> p v k"), ctan.rearrange("p (v k) -> p v k", v=4),
                              0.5, None, ALU.mult).then_inc(S["cond_ready"], 1)
            dve.wait_ge(S["start_act"], 1)
            step(dve.tensor_scalar(sp_w, sp_z, 2.0, None, ALU.add))
            step(dve.reciprocal(sp_w, sp_w))
            step(dve.tensor_tensor(sp_w, sp_w, sp_z, ALU.mult))
            step(dve.tensor_tensor(sp_z, sp_w, sp_w, ALU.mult))
            step(dve.tensor_scalar(sp_r, sp_z, LOG1P[0], None, ALU.mult))
            for c in LOG1P[1:]:
                step(dve.scalar_tensor_tensor(out=sp_r, in0=sp_r, scalar=c, in1=sp_z, op0=ALU.add, op1=ALU.mult))
            step(dve.scalar_tensor_tensor(out=sp_r, in0=sp_r, scalar=1.0, in1=sp_w, op0=ALU.add, op1=ALU.mult))
            step(dve.scalar_tensor_tensor(out=sp_r, in0=sp_r, scalar=2.0, in1=sp_n, op0=ALU.mult, op1=ALU.add))
            dve.tensor_scalar(sp4, sp_r, 4.0, None, ALU.mult)
            step(dve.tensor_scalar(neg_sp4, sp_r, -4.0, None, ALU.mult))
            dve.wait_ge(S["start_act"], 2)
            step(dve.tensor_tensor(lam_col, lam_e[:, 0:1], lam_e[:, 1:2], ALU.subtract))
            step(dve.tensor_scalar(lam_col, lam_col, LAM_INIT, None, ALU.add))
            with dve.Fori(0, MOD_FIRST) as m:
                mod_add(dve, m)

        def start_pe(pe):
            pe.wait_ge(S["consts_in"], 16)
            pe.wait_ge(S["start_dve"], 1)
            pe.matmul(psum[:, 0, 0:2], ones, lam_p, start=True, stop=True).then_inc(S["start_pe"], 1)
            pe.wait_ge(S["cond_ready"], 1)

            def group(m):
                for q in range(4):
                    mod_chunk(pe, m, q)
                mod_turn(pe, m, 0)
            group(0)
            with pe.Fori(1, MOD_FIRST) as m:
                group(m)

        block = ctx.enter_context(nc.Block())

        @block.sync
        def _(sp):
            sp.dma_start(cols[:, :], ins["cols"]).then_inc(S["cols_in"], 16)
            sp.dma_start(consts[:, :], ins["consts"]).then_inc(S["consts_in"], 16)
            x_t = ins["x_t"].rearrange("k p t -> p k t")
            sp.dma_start(xl[:, :, :], x_t[:, :, 0:T]).then_inc(S["x_in"], 16)
            sp.dma_start(y[:, 1, :, :], x_t[:, :, T:NT]).then_inc(S["x_in"], 16)
            for par in range(2):
                load_strip(sp, 0, par, True)
            with sp.Fori(1, N_STRIPS // 2) as pair:
                for par in range(2):
                    load_strip(sp, pair, par)
            sp.wait_ge(S["x_new"], 4 * KT)
            sp.dma_start(out.rearrange("k p t -> p k t"), xl[:, :, :]).then_inc(S["out_stored"], 16)
            sp.wait_ge(S["out_stored"], 16)

        @block.gpsimd
        def _(pool):
            start_pool(pool)
            for q in range(4):
                mod_load(pool, 0, q, q < 2)
            with pool.Fori(1, MOD_FIRST) as m:
                for q in range(4):
                    mod_load(pool, m, q)
            norm_pool(pool, 0)
            lru_pool(pool)
            out_pool(pool, 0)
            norm_pool(pool, 1)
            att_pool(pool)
            pool.wait_ge(A["att_y"], HEADS1)
            pool.dma_start(y[:, 1, :, :], ins["ctx2_t"].rearrange("k p t -> p k t")).then_inc(S["ctx2_in"], 16)
            out_pool(pool, 1)
            for lay in range(2):
                norm_pool(pool, 2 + lay)
                sgu_pool(pool, lay)
                out_pool(pool, 2 + lay)

        @block.scalar
        def _(act):
            start_act(act)
            for c in range(2):
                split_hi(act, 0, c)
            norm_act(act, 0)
            lru_act(act)
            out_act(act, 0)
            norm_act(act, 1)
            att_act(act)
            out_act(act, 1)
            for lay in range(2):
                norm_act(act, 2 + lay)
                sgu_act(act, lay)
                kv_act(act, lay)
                gqa_act(act, lay)
                out_act(act, 2 + lay)

        @block.vector
        def _(dve):
            start_dve(dve)
            for c in range(2):
                split_lo(dve, 0, c)
            norm_dve(dve, 0)
            lru_dve(dve)
            out_dve(dve, 0)
            norm_dve(dve, 1)
            att_dve(dve)
            out_dve(dve, 1)
            for lay in range(2):
                norm_dve(dve, 2 + lay)
                sgu_dve(dve, lay)
                kv_dve(dve, lay)
                gqa_dve(dve, lay)
                out_dve(dve, 2 + lay)

        @block.tensor
        def _(pe):
            start_pe(pe)
            norm_pe(pe, 0)
            lru_pe(pe)
            out_pe(pe, 0)
            norm_pe(pe, 1)
            att_pe(pe)
            out_pe(pe, 1)
            for lay in range(2):
                norm_pe(pe, 2 + lay)
                sgu_pe(pe, lay)
                kv_pe(pe, lay)
                gqa_pe(pe, lay)
                out_pe(pe, 2 + lay)


def _strips(w, columns):
    tiles = w.reshape(KT, P, -1, P)[:, :, columns, :]
    tiles = tiles.reshape(2, HALF, P, len(columns), P).transpose(3, 0, 2, 1, 4)
    return np.ascontiguousarray(tiles).reshape(2 * len(columns), P, HALF * P)


def _stream(i):
    parts = [
        _strips(i["lru_w_in"][0], [c for b in range(BLOCKS) for c in (b, BLOCKS + b)]),
        _strips(i["lru_w_out"][0], list(range(KT))),
        _strips(i["att_w_in"][0], [c for h in range(HEADS1) for c in (HEADS1 + h, h, 2 * HEADS1 + h, 3 * HEADS1 + h)]),
        _strips(i["att_w_out"][0], list(range(KT))),
    ]
    u, v, z, q, k, zb = 0, 8, 16, 24, 32, 36
    heads = [kv * REP2 + r for r in range(REP2) for kv in range(KV2)]
    order = ([c for g in range(GROUPS) for c in (u + g, v + g, z + g)] + [k, k + 1, k + 2, k + 3]
             + [c for h in heads for c in (q + h, zb + h)])
    for lay in range(2):
        parts += [_strips(i["w_in_2"][lay], order), _strips(i["w_out_2"][lay], list(range(KT)))]
    return np.concatenate(parts)


def _mod_stream(i):
    w = np.concatenate([i["mod_w"], i["w_mod_2"]]).reshape(4, 4, 4, P, 12, 512)
    return np.ascontiguousarray(w.transpose(0, 4, 1, 3, 2, 5)).reshape(4 * MOD_GROUPS, P, 4, 512)


def _columns(i):
    def f(a):
        return a.reshape(-1, P).T
    qk1 = np.concatenate([np.tile(i[n][0], 2)[:, None] for n in ("att_q_norm", "att_k_norm")], axis=1)
    att_lam = np.zeros((P, 4), np.float32)
    att_lam[:HD1] = i["att_lambda"][0].T
    parts = dict(
        c=f(np.concatenate([i["c"].ravel(), i["c_ctx"], i["c_2"].ravel(), i["c_ctx_2"]])),
        norm_g=f(np.concatenate([i["norm_g"], i["norm_w_2"]])),
        mod_b=f(np.concatenate([i["mod_b"], i["b_mod_2"]])),
        conv_w=f(i["lru_conv_w"][0].reshape(4, BLOCKS, P).transpose(1, 0, 2)),
        conv_b=f(i["lru_conv_b"][0]),
        gate_b=f(i["lru_gate_b"][0].transpose(2, 0, 1, 3)),
        lam=f(i["lru_lambda"][0].reshape(2, BLOCKS, P).transpose(1, 0, 2)),
        v_norm=f(i["v_norm_w_2"]),
        qk2=f(np.concatenate([i["q_norm_w_2"], i["k_norm_w_2"]])),
        qk1=qk1, subln=f(i["att_subln"]), att_lam=att_lam)
    return np.ascontiguousarray(np.concatenate([parts[n] for n in _widths], axis=1))


def _constants():
    f = np.float32
    same = np.kron(np.eye(2), np.ones((HD1, HD1)))

    def rotation(half):
        r = np.zeros((P, P))
        for d in range(P):
            if d % (2 * half) < half:
                r[d + half, d] = -1.0
            else:
                r[d - half, d] = 1.0
        return r
    sel = np.zeros((2, P, 2))
    for net in range(2):
        for j in range(4):
            for s in range(2):
                sel[net, 32 * j + 2 * net + s, s] = 1.0
    row, colm = (np.arange(T) // 64).astype(f), (np.arange(T) % 64).astype(f)

    def tables(freqs, copies):
        inv = (f(10000.0) ** (-np.arange(freqs, dtype=f) / f(freqs))).astype(f)
        ang = np.concatenate([np.tile(pos[None, :] * inv[:, None], (2, 1)) for pos in (row, colm)])
        ang = np.tile(ang, (copies, 1)).astype(f)
        return [np.cos(ang), np.sin(ang)]
    parts = [np.eye(P), np.ones((P, P)), same, rotation(16), rotation(32), sel[0], sel[1]]
    parts += tables(16, 2) + tables(32, 1)
    return np.ascontiguousarray(np.concatenate(parts, axis=1).astype(f))


def kernel(**inputs):
    import concourse.bacc as bacc
    from concourse.bass_utils import run_bass_kernel_spmd

    i = {n: np.asarray(a) for n, a in inputs.items()}

    def feature_major(x):
        return x.reshape(T, KT, P).transpose(1, 2, 0)
    b = np.broadcast_to(i["b_sgu_2"].reshape(2 * GROUPS, 1, P), (2 * GROUPS, P, P))
    arrays = {
        "weights": _stream(i),
        "mod_weights": _mod_stream(i),
        "cols": _columns(i),
        "consts": _constants(),
        "x_t": np.ascontiguousarray(np.concatenate([feature_major(i["x"]), feature_major(i["ctx"])], axis=2)),
        "ctx2_t": np.ascontiguousarray(feature_major(i["ctx_2"])),
        "gate_w": np.ascontiguousarray(i["lru_gate_w"][0].transpose(2, 3, 0, 1, 4)).reshape(BLOCKS, P, 4 * P),
        "sgu_tab": np.ascontiguousarray(np.concatenate(
            [i["w_sgu_2"].reshape(2 * GROUPS, P, P).transpose(0, 2, 1), b], axis=2)),
    }
    nc = bacc.Bacc("TRN2", target_bir_lowering=False, num_devices=1)
    ins = {n: nc.dram_tensor("in_" + n, a.shape, mybir.dt.from_np(a.dtype), kind="ExternalInput").ap()
           for n, a in arrays.items()}
    out = nc.dram_tensor("out_t", (KT, P, T), F32, kind="ExternalOutput").ap()
    build(nc, ins, out)
    r = run_bass_kernel_spmd(nc, [{"in_" + n: a for n, a in arrays.items()}], core_ids=[0])
    return np.ascontiguousarray(r.results[0]["out_t"].transpose(2, 0, 1)).reshape(1, T, D)
```

```python
from contextlib import ExitStack
import math

import numpy as np
import concourse.bass as bass
from concourse import mybir

F32 = mybir.dt.float32
F32R = mybir.dt.float32r
ALU = mybir.AluOpType
ACT = mybir.ActivationFunctionType
AX_X = mybir.AxisListType.X

P = 128
D = 2048
KT = D // P
T = 256
NT = 2 * T
TT = T // P
EPS = 1e-6
HALF = KT // 2

BLOCKS = 16
HEADS1 = 16
HD1 = 64
LAM_INIT = 0.8 - 0.6 * math.exp(-0.3)
GROUPS = 8
HEADS2 = 8
KV2 = 2
REP2 = HEADS2 // KV2
SCALE2 = float(P) ** -0.5

S_LRU = 0
S_LRU_OUT = S_LRU + 2 * BLOCKS
S_ATT = S_LRU_OUT + KT
S_ATT_OUT = S_ATT + 4 * HEADS1
S_NET2 = S_ATT_OUT + KT
L2_KV = 3 * GROUPS
L2_ATT = L2_KV + 2 * KV2
L2_OUT = L2_ATT + 2 * HEADS2
L2_STRIPS = L2_OUT + KT
N_STRIPS = S_NET2 + 2 * L2_STRIPS

MOD_GROUPS = 48
MOD_FIRST = 8
M_LRU = MOD_FIRST
M_ATT = M_LRU + BLOCKS
M_SGU = M_ATT + HEADS1

_widths = dict(c=4 * KT, norm_g=4 * KT, mod_b=4 * 48, conv_w=4 * BLOCKS, conv_b=BLOCKS, gate_b=4 * BLOCKS,
               lam=2 * BLOCKS, v_norm=2 * GROUPS, qk2=4, qk1=2, subln=1, att_lam=4)
COL, _at = {}, 0
for _n, _w in _widths.items():
    COL[_n] = (_at, _at + _w)
    _at += _w
N_COLS = _at


def build(nc, ins, out):
    with ExitStack() as ctx:
        def sb(name, shape, dt=F32):
            return ctx.enter_context(nc.sbuf_tensor(name, shape, dt))

        def sems(phase, names):
            return {n: ctx.enter_context(nc.semaphore(phase + n)) for n in names.split()}

        xl = sb("xl", [P, KT, T])
        y = sb("y", [P, 2, KT, T])
        h_hi = sb("h_hi", [P, KT, NT], F32R)
        h_lo = sb("h_lo", [P, KT, NT], F32R)
        raw = sb("raw", [P, 4, HALF * P])
        w_hi = sb("w_hi", [P, 2, 2, HALF * P], F32R)
        w_lo = sb("w_lo", [P, 2, 2, HALF * P], F32R)
        modraw = sb("modraw", [P, 2, 4, 512])
        mod = sb("mod", [P, 192, 2])
        cols = sb("cols", [P, N_COLS])
        cond = sb("cond", [P, KT, 32])
        consts = sb("consts", [P, 5 * P + 4 + 4 * T])
        small = sb("small", [P, 256])
        modrow = sb("modrow", [P, 512])
        WORK = 4288
        work = sb("work", [P, WORK])
        psum = ctx.enter_context(nc.psum_tensor("psum", [P, 8, 512], F32))

        ident, ones = consts[:, 0:P], consts[:, P:2 * P]
        ones64, rot1, rot2 = (consts[:, n * P:(n + 1) * P] for n in (2, 3, 4))
        sel = [consts[:, 5 * P + 2 * n:5 * P + 2 * n + 2] for n in range(2)]
        tab = 5 * P + 4
        cos1, sin1, cos2, sin2 = (consts[:, tab + n * T:tab + (n + 1) * T] for n in range(4))

        def col(name, a, n=1):
            return cols[:, bass.ds(COL[name][0] + a, n)]

        class Space:

            def __init__(self, *parts):
                self.parts = [[p, n, 0] for p, n in parts]

            def __call__(self, n):
                for part in self.parts:
                    if part[2] + n <= part[1]:
                        part[2] += n
                        return part[0][:, part[2] - n:part[2]]
                raise ValueError("work space")

        work_all = (work, WORK)
        xl_all = (xl[:, :, :].rearrange("p k t -> p (k t)"), KT * T)
        yc_all = (y[:, 1, :, :].rearrange("p k t -> p (k t)"), KT * T)
        modraw_all = (modraw[:, :, :, :].rearrange("p a b c -> p (a b c)"), 4096)

        def two(ap):
            return ap.rearrange("p (s t) -> p s t", s=2)

        _small_at = [0]

        def tiny(n):
            _small_at[0] += n
            assert _small_at[0] <= 256
            return small[:, _small_at[0] - n:_small_at[0]]

        neg_sp4, sp4 = tiny(2 * BLOCKS), tiny(2 * BLOCKS)
        half_gb = tiny(4 * BLOCKS)
        qg1, subg, lam_col = tiny(1), tiny(1), tiny(1)
        mod_a = tiny(2 * KT).rearrange("p (k s) -> p k s", s=2)
        eps_col, warm = tiny(1), tiny(1)
        rcol = tiny(NT // P)

        S = sems(
            "", "consts_in cols_in x_in ctx2_in raw_in0 raw_in1 raw_in2 raw_in3 split_hi split_lo strip_done "
            "first_in0 first_in1 first_in2 first_in3 modraw_in0 modraw_in1 mod_used modrow_ready modcol_ps mod_cols "
            "pads_zero cond_tanh cond_ready start_dve start_act start_pe start_tab "
            "xa_done rcol_done rstd_ps mod_a_done xn_done sq_done sq_added ss_done sd_done rstd_done t_done hf_done hhi_done h_ready "
            "y_hi y_ready res_in0 res_in1 x_new out_stored "
        )
        raw_in = [S["raw_in0"], S["raw_in1"], S["raw_in2"], S["raw_in3"]]
        first_in = [S[f"first_in{q}"] for q in range(4)]
        modraw_in = [S["modraw_in0"], S["modraw_in1"]]
        res_in = [S["res_in0"], S["res_in1"]]
        L = sems("lru_", "gw_in0 gw_in1 u_evac conv_step xc_ready tg_done silu_done gate_done gates_tanh coef_step "
                 "coef_done m_done sqrt_done bx_done b_done scan_done ysum_done lru_y")
        gw_in = [L["gw_in0"], L["gw_in1"]]
        A = sems("att_", "k_evac q_evac v_evac tg sgl ssk ssq sso sdk sdq sdo rsk rsq rso kn qn rotk rotq kt1 kr qt1 qr "
                 "scores smax negmax expd rsum p1s attn attn_t attn_sb v_t v_sb av o_evac on att_y")
        G = sems("sgu_", "tab_in0 tab_in1 gu gv tz sz v_t sqv ssv sdv rsv vn s sb1 sb2 gu_y")
        B = sems("gqa_", "k_evac v_evac ssk sdk rsk kn rotk kt1 kr v_t v_sb "
                 "q_evac tz sz ssq sdq rsq qn rotq qt1 qr scores smax negmax expd rsum attn attn_t attn_sb av y2")

        def ge(eng, sem, value):
            if not (isinstance(value, int) and value <= 0):
                eng.wait_ge(sem, value)

        class Chain:

            def __init__(self, eng, sem, done, per):
                self.eng, self.sem, self.done, self.per, self.n = eng, sem, done, per, 0

            def __call__(self, ins):
                self.n += 1
                ins.then_inc(self.sem, 1)
                self.eng.wait_ge(self.sem, self.done + self.n)

            def close(self):
                assert self.n == self.per, (self.n, self.per)

        class Strip:

            def __init__(self, base, c, j=0, per=2):
                assert base % 2 == 0 and per % 2 == 0
                self.pair, self.par = (base + c) // 2 + (per // 2) * j, c % 2
                self.s = 2 * self.pair + self.par

        def load_strip(sp, pair, par, first=False):
            s = 2 * pair + par
            for half in range(2):
                if not first:
                    sp.wait_ge(S["split_lo"], 2 * (s - 2) + half + 1)
                sp.dma_start(raw[:, 2 * par + half, :], ins["weights"][2 * s + half]).then_inc(raw_in[2 * par + half], 16)

        def split_hi(act, pair, par, halves=(0, 1)):
            s = 2 * pair + par
            for half in halves:
                act.wait_ge(raw_in[2 * par + half], 16 * (pair + 1))
                if half == 0:
                    ge(act, S["strip_done"], s - 1)
                act.activation(w_hi[:, par, half, :], raw[:, 2 * par + half, :], ACT.Copy).then_inc(S["split_hi"], 1)

        def split_lo(dve, pair, par, halves=(0, 1)):
            s = 2 * pair + par
            for half in halves:
                dve.wait_ge(S["split_hi"], 2 * s + half + 1)
                if half == 0:
                    ge(dve, S["strip_done"], s - 1)
                dve.tensor_tensor(w_lo[:, par, half, :], raw[:, 2 * par + half, :],
                                  w_hi[:, par, half, :].bitcast(F32), ALU.subtract).then_inc(S["split_lo"], 1)

        def next_strip(split, eng, st):
            if not (isinstance(st.pair, int) and 2 * st.pair + st.par + 2 >= N_STRIPS):
                split(eng, st.pair + 1, st.par)

        def strip(pe, st, dst, n, between=None, operand=None):
            for half in range(2):
                pe.wait_ge(S["split_lo"], 2 * st.s + half + 1)
                for kk in range(HALF):
                    k = half * HALF + kk
                    if operand is not None:
                        pe.wait_ge(operand[0], operand[1] + k + 1)
                    hi, lo = (w[:, st.par, half, kk * P:(kk + 1) * P] for w in (w_hi, w_lo))
                    pe.matmul(dst, hi, h_hi[:, k, 0:n], start=(k == 0), stop=False)
                    pe.matmul(dst, hi, h_lo[:, k, 0:n], start=False, stop=False)
                    mm = pe.matmul(dst, lo, h_hi[:, k, 0:n], start=False, stop=(k == KT - 1))
                if half == 1:
                    mm.then_inc(S["strip_done"], 1)
                if between is not None:
                    between(half)

        pmod = psum[:, 7, :]

        def mod_products(pe, bank, chunk, q):
            for j in range(4):
                mm = pe.matmul(bank[32 * j:32 * j + 32, :], cond[:, 4 * q + j, :], chunk[:, j, :],
                               start=(q == 0), stop=(q == 3))
            mm.then_inc(S["mod_used"], 1)

        def mod_load(pool, m, q):
            pool.wait_ge(S["mod_used"], 4 * m + q - 1)
            pool.dma_start(modraw[:, q % 2, :, :], ins["mod_weights"][4 * m + q]).then_inc(modraw_in[q % 2], 16)

        def mod_chunk(pe, m, q):
            pe.wait_ge(modraw_in[q % 2], 16 * (2 * (m - MOD_FIRST) + q // 2 + 1))
            if q == 0:
                pe.wait_ge(S["mod_cols"], m)
            mod_products(pe, pmod, modraw[:, q % 2, :, :], q)

        def mod_rows(act, m, bank=pmod):
            act.wait_ge(S["mod_used"], 4 * m + 4)
            ge(act, S["modcol_ps"], m)
            act.activation(modrow[:, :], bank, ACT.Copy).then_inc(S["modrow_ready"], 1)

        def mod_turn(pe, m, net, bank=pmod):
            pe.wait_ge(S["modrow_ready"], m + 1)
            for b in range(4):
                mm = pe.matmul(bank[:, 2 * b:2 * b + 2], modrow[:, b * P:(b + 1) * P], sel[net], start=True, stop=True)
            mm.then_inc(S["modcol_ps"], 1)

        def mod_add(dve, m, bank=pmod, at=None):
            at = m if at is None else at
            dve.wait_ge(S["modcol_ps"], m + 1)
            dve.tensor_tensor(mod[:, bass.ds(4 * at, 4), :], bank[:, 0:8].rearrange("p (b s) -> p b s", s=2),
                              col("mod_b", 4 * at, 4).unsqueeze(2).to_broadcast([P, 4, 2]), ALU.add).then_inc(S["mod_cols"], 1)

        def normalize_bufs(space):
            return dict(rstd=space(NT), t=[space(NT) for _ in range(2)], hf=[space(NT) for _ in range(2)])

        w0 = Space(work_all)
        acc = w0(NT)
        sqb = [w0(NT), w0(NT)]
        res = [w0(NT), w0(NT)]
        nb = normalize_bufs(Space((work[:, NT:WORK], WORK - NT)))
        SS_BANK = 6
        added_base = [(KT - 2) * l for l in range(5)]

        hs4 = nb["hf"] + nb["t"]

        def norm_pe(pe, l):
            pe.wait_ge(S["sq_added"], added_base[l + 1])
            for n, sq in enumerate((acc, sqb[0], sqb[1])):
                if n > 0:
                    pe.wait_ge(S["sq_done"], KT * (l + 1) - 2 + n)
                for t in range(NT // P):
                    mm = pe.matmul(psum[:, SS_BANK, t:t + 1], sq[:, t * P:(t + 1) * P], ones[:, 0:1],
                                   start=(n == 0 and t == 0), stop=(n == 2 and t == NT // P - 1))
            mm.then_inc(S["ss_done"], 1)
            pe.wait_ge(S["rcol_done"], l + 1)
            for t in range(NT // P):
                mm = pe.matmul(psum[:, SS_BANK, t * P:(t + 1) * P], rcol[:, t:t + 1].to_broadcast([P, P]), ident,
                               start=True, stop=True)
            mm.then_inc(S["rstd_ps"], 1)

        def norm_sqrt(act, l):
            act.wait_ge(S["ss_done"], l + 1)
            act.activation(rcol, psum[:, SS_BANK, 0:NT // P], ACT.Sqrt, scale=1.0 / D, bias=eps_col).then_inc(S["sd_done"], 1)
            if l > 0:
                split_hi(act, layer_strip[l] // 2, 1, halves=(0,))
            act.wait_ge(S["rstd_ps"], l + 1)
            act.activation(nb["rstd"], psum[:, SS_BANK, :], ACT.Copy).then_inc(S["rstd_done"], 1)
            if l > 0:
                split_hi(act, layer_strip[l] // 2, 1, halves=(1,))

        def norm_reciprocal(dve, l):
            dve.wait_ge(S["sd_done"], l + 1)
            dve.reciprocal(rcol, rcol).then_inc(S["rcol_done"], 1)

        def norm_act(act, l):
            norm_sqrt(act, l)
            act.wait_ge(S["strip_done"], layer_strip[l])
            with act.Fori(0, KT // 4) as j:
                for c in range(4):
                    k = 4 * j + c
                    act.wait_ge(S["t_done"], KT * (l - 1) + k + 1)
                    act.wait_ge(S["hf_done"], KT * l + k + 1)
                    for s in range(2):
                        ins_ = act.activation(h_hi[:, k, s * T:(s + 1) * T], hs4[c][:, s * T:(s + 1) * T], ACT.Identity,
                                              bias=mod[:, bass.ds(48 * l + k, 1), s])
                    ins_.then_inc(S["hhi_done"], 1)

        def norm_pool(pool, l):
            pool.wait_ge(S["xa_done"], KT * l)
            pool.wait_ge(S["rstd_done"], l + 1)
            with pool.Fori(0, KT // 4) as j:
                for c in range(4):
                    k = 4 * j + c
                    pool.wait_ge(S["h_ready"], KT * l + k - 3)
                    pool.tensor_tensor(hs4[c][:, 0:T], y[:, 0, k, :], nb["rstd"][:, 0:T], ALU.mult).then_inc(S["t_done"], 1)

        def norm_dve(dve, l):
            norm_reciprocal(dve, l)
            split_lo(dve, layer_strip[l] // 2, 1, halves=(0,))
            dve.wait_ge(S["mod_a_done"], MOD_FIRST // 2 + l)
            dve.wait_ge(S["rstd_done"], l + 1)
            dve.wait_ge(S["strip_done"], layer_strip[l])

            def context(k, c):
                dve.wait_ge(S["h_ready"], KT * l + k - 3)
                dve.scalar_tensor_tensor(out=hs4[c][:, T:NT], in0=y[:, 1, k, :], scalar=mod_a[:, bass.ds(k, 1), 1],
                                         in1=nb["rstd"][:, T:NT], op0=ALU.mult, op1=ALU.mult).then_inc(S["hf_done"], 1)

            def low(k, c):
                dve.wait_ge(S["hhi_done"], KT * l + k + 1)
                for s in range(2):
                    part = slice(s * T, (s + 1) * T)
                    ins_ = dve.scalar_tensor_tensor(out=h_lo[:, k, part], in0=hs4[c][:, part], scalar=mod[:, bass.ds(48 * l + k, 1), s],
                                                    in1=h_hi[:, k, part].bitcast(F32), op0=ALU.add, op1=ALU.subtract)
                ins_.then_inc(S["h_ready"], 1)
            context(0, 0)
            context(1, 1)
            split_lo(dve, layer_strip[l] // 2, 1, halves=(1,))
            with dve.Fori(0, KT // 4 - 1) as j:
                for c in range(4):
                    low(4 * j + c, c)
                    context(4 * j + c + 2, (c + 2) % 4)
            for c in range(4):
                low(KT - 4 + c, c)
                if c < 2:
                    context(KT - 2 + c, c + 2)

        layer_strip = [S_LRU, S_ATT, S_NET2, S_NET2 + L2_STRIPS]
        out_strip = [S_LRU_OUT, S_ATT_OUT, S_NET2 + L2_OUT, S_NET2 + L2_STRIPS + L2_OUT]
        wide = [True, False, True, False]
        n_of = [NT if w else T for w in wide]
        fetched = [0, 2]
        y_sem = [L["lru_y"], A["att_y"], B["y2"], B["y2"]]
        y_count = [BLOCKS, HEADS1, HEADS2, 2 * HEADS2]

        def y_view(l, k):
            return y[:, :, k, :] if wide[l] else y[:, 0, k, :]

        def h_view(h, l, k):
            return two(h[:, k, :]) if wide[l] else h[:, k, 0:T]

        OUT_REST = KT - 1
        OUT_REST2 = KT - 6

        def to_high(act, l, k0, k1):
            if k0 == 0:
                act.wait_ge(S["strip_done"], out_strip[l])
            for k in range(k0, k1):
                if l < 2:
                    act.wait_ge(y_sem[l], k + 1)
                elif k < GROUPS:
                    act.wait_ge(G["gu_y"], GROUPS * (l - 2) + k + 1)
                else:
                    act.wait_ge(B["y2"], HEADS2 * (l - 2) + k - GROUPS + 1)
                act.activation(h_view(h_hi, l, k), y_view(l, k), ACT.Copy).then_inc(S["y_hi"], 1)

        def to_low(dve, l, k0, k1):
            for k in range(k0, k1):
                dve.wait_ge(S["y_hi"], KT * l + k + 1)
                dve.tensor_tensor(h_view(h_lo, l, k), y_view(l, k), h_view(h_hi, l, k).bitcast(F32),
                                  ALU.subtract).then_inc(S["y_ready"], 1)

        def out_first(pe, l, k0, k1, strips=(0, 1)):
            n = n_of[l]
            for k in range(k0, k1):
                half, kk = divmod(k, HALF)
                if kk == 0:
                    pe.wait_ge(S["split_lo"], 2 * (out_strip[l] + 1) + half + 1)
                pe.wait_ge(S["y_ready"], KT * l + k + 1)
                for c in strips:
                    if c == 1 and len(strips) == 2 and k >= OUT_REST2:
                        continue
                    hi, lo = (w[:, c, half, kk * P:(kk + 1) * P] for w in (w_hi, w_lo))
                    pe.matmul(psum[:, c, 0:n], hi, h_hi[:, k, 0:n], start=(k == 0), stop=False)
                    pe.matmul(psum[:, c, 0:n], hi, h_lo[:, k, 0:n], start=False, stop=False)
                    mm = pe.matmul(psum[:, c, 0:n], lo, h_hi[:, k, 0:n], start=False, stop=(k == KT - 1))
                    if k == KT - 1:
                        mm.then_inc(S["strip_done"], 1)

        def out_pe(pe, l):
            n = n_of[l]
            out_first(pe, l, OUT_REST, KT, strips=(0,))
            out_first(pe, l, OUT_REST2, KT, strips=(1,))
            with pe.Fori(1, KT // 2) as j:
                for c in range(2):
                    st = Strip(out_strip[l], c, j)
                    pe.wait_ge(S["x_new"], KT * l + 2 * j + c - 1)
                    strip(pe, st, psum[:, c, 0:n], n)

        def out_act(act, l):
            to_high(act, l, OUT_REST, KT)

            def squares(j, c):
                m = 2 * j + c
                act.wait_ge(S["x_new"], KT * l + m + 1)
                if not (isinstance(j, int) and j == 0):
                    act.wait_ge(S["sq_added"], added_base[l + 1] + m - 1)
                if not wide[l]:
                    act.wait_ge(S["ctx2_in"], 16)
                act.activation(sqb[c][:, 0:T], xl[:, m, :], ACT.Square)
                act.activation(sqb[c][:, T:NT], y[:, 1, m, :], ACT.Square).then_inc(S["sq_done"], 1)

            def tile(j, c, last):
                st = Strip(out_strip[l], c, j)
                near_end = isinstance(j, int) and j == KT // 2 - 1
                last = last or near_end and c == 1
                if near_end and l < 3:
                    squares(j, c)
                act.wait_ge(S["strip_done"], st.s + 1)
                if not last:
                    next_strip(split_hi, act, st)
                if not near_end and l < 3:
                    squares(j, c)
            for c in range(2):
                tile(0, c, False)
            with act.Fori(1, KT // 2 - 1) as j:
                for c in range(2):
                    tile(j, c, False)
            if l < 3:
                act.activation(warm, eps_col, ACT.Sqrt)
            for c in range(2):
                tile(KT // 2 - 1, c, l == 3)

        def out_pool(pool, l):
            def fetch(m, c, first):
                if not first:
                    pool.wait_ge(S["x_new"], KT * l + m - 1)
                if l == 0:
                    pool.dma_start(res[c], ins["x_t"][m]).then_inc(res_in[c], 16)
                else:
                    pool.dma_start(res[c][:, T:NT], ins["ctx2_t"][m]).then_inc(res_in[c], 16)

            def add(m, c, first):
                pool.wait_ge(S["sq_done"], KT * (l + 1) + m + 1)
                if first:
                    pool.tensor_copy(acc, sqb[c]).then_inc(S["sq_added"], 1)
                elif not isinstance(m, int) or m < KT - 2:
                    pool.wait_ge(S["sq_added"], added_base[l + 1] + m)
                    pool.tensor_tensor(acc, acc, sqb[c], ALU.add).then_inc(S["sq_added"], 1)
                pool.tensor_tensor(y[:, 0, m, :], xl[:, m, :], mod_a[:, bass.ds(m, 1), 0].to_broadcast([P, T]),
                                   ALU.mult).then_inc(S["xa_done"], 1)
            if l in fetched:
                pool.wait_ge(y_sem[l], y_count[l])
                for c in range(2):
                    fetch(c, c, True)
            if l < 3:
                pool.wait_ge(S["mod_a_done"], MOD_FIRST // 2 + l + 1)
                for c in range(2):
                    add(c, c, c == 0)
                    if l in fetched:
                        fetch(2 + c, c, False)
                with pool.Fori(1, KT // 2 - 1) as j:
                    for c in range(2):
                        add(2 * j + c, c, False)
                        if l in fetched:
                            fetch(2 * j + 2 + c, c, False)
                for c in range(2):
                    add(KT - 2 + c, c, False)

        def out_dve(dve, l):
            nth = fetched.index(l) if l in fetched else 0
            to_low(dve, l, OUT_REST, KT)
            dve.wait_ge(S["mod_cols"], min(12 * l + 20, MOD_GROUPS))
            dve.wait_ge(S["y_ready"], KT * (l + 1))
            if l < 3:
                dve.wait_ge(S["h_ready"], KT * (l + 1))
                dve.scalar_tensor_tensor(
                    out=mod_a, in0=mod[:, 48 * l + 64:48 * l + 80, :], scalar=1.0,
                    in1=col("norm_g", KT * (l + 1), KT).unsqueeze(2).to_broadcast([P, KT, 2]),
                    op0=ALU.add, op1=ALU.mult).then_inc(S["mod_a_done"], 1)

            def tile(j, c, last):
                st = Strip(out_strip[l], c, j)
                m = 2 * j + c
                dve.wait_ge(S["strip_done"], st.s + 1)
                if l in fetched:
                    dve.wait_ge(res_in[c], 16 * (KT // 2 * nth + j + 1))
                gate = lambda s: mod[:, bass.ds(48 * l + 32 + m, 1), s]
                if wide[l]:
                    dve.scalar_tensor_tensor(out=y[:, 1, m, :], in0=psum[:, c, T:NT], scalar=gate(1),
                                             in1=res[c][:, T:NT], op0=ALU.mult, op1=ALU.add)
                dve.scalar_tensor_tensor(out=xl[:, m, :], in0=psum[:, c, 0:T], scalar=gate(0),
                                         in1=res[c][:, 0:T] if l == 0 else xl[:, m, :],
                                         op0=ALU.mult, op1=ALU.add).then_inc(S["x_new"], 1)
                if not last:
                    next_strip(split_lo, dve, st)
            with dve.Fori(0, KT // 2 - 1) as j:
                for c in range(2):
                    tile(j, c, False)
            for c in range(2):
                tile(KT // 2 - 1, c, l == 3 or c == 1)

        lsp = Space(xl_all, work_all)
        upad = lsp(2 * 260).rearrange("p (s t) -> p s t", s=2)
        lw = dict(
            tr=[lsp(NT), lsp(NT)], ti=[lsp(NT), lsp(NT)], a=[lsp(NT), lsp(NT)], th=[lsp(NT), lsp(NT)],
            xc=lsp(NT), sg=lsp(NT), gw=[lsp(4 * P).rearrange("p (g d) -> p g d", g=4) for _ in range(2)])
        U_BANK, G_BANK, GATE_BANK = 0, 1, 2
        CONV_W = 4

        def lru_pool(pool):
            def block(b, par, first):
                if not first:
                    pool.wait_ge(L["gate_done"], 4 * (b - 1))
                pool.dma_start(lw["gw"][par], ins["gate_w"][b].rearrange("p (g d) -> p g d", g=4)).then_inc(gw_in[par], 16)
                for q in range(2 if isinstance(b, int) and b == 0 else 0, 4):
                    mod_load(pool, M_LRU + b, q)
            for q in range(2):
                mod_load(pool, M_LRU, q)
            pool.wait_ge(S["hf_done"], KT)
            pool.wait_ge(S["h_ready"], KT)
            for b in range(2):
                block(b, b, True)
            with pool.Fori(1, BLOCKS // 2) as j:
                for par in range(2):
                    block(2 * j + par, par, False)

        def lru_pe(pe):
            def block(j, par, first=False):
                b = 2 * j + par
                su, sg = Strip(S_LRU, 2 * par, j, 4), Strip(S_LRU, 2 * par + 1, j, 4)
                ge(pe, L["u_evac"], b)
                strip(pe, su, psum[:, U_BANK, :], NT, between=lambda half: mod_chunk(pe, M_LRU + b, half),
                      operand=(S["h_ready"], 0) if first else None)
                ge(pe, L["silu_done"], b)
                strip(pe, sg, psum[:, G_BANK, :], NT, between=lambda half: mod_chunk(pe, M_LRU + b, 2 + half))
                pe.wait_ge(L["xc_ready"], b + 1)
                pe.wait_ge(gw_in[par], 16 * (j + 1))
                for g in range(4):
                    ge(pe, L["gates_tanh"], 4 * (b - 1) + g + 1)
                    pe.matmul(psum[:, GATE_BANK + g, :], lw["gw"][par][:, g, :], lw["xc"], start=True, stop=True).then_inc(L["gate_done"], 1)
                mod_turn(pe, M_LRU + b, 0)
            block(0, 0, True)
            block(0, 1)
            with pe.Fori(1, BLOCKS // 2 - 1) as j:
                for par in range(2):
                    block(j, par)
            for par in range(2):
                block(BLOCKS // 2 - 1, par)
            pe.wait_ge(L["u_evac"], BLOCKS)
            pe.wait_ge(L["silu_done"], BLOCKS)
            out_first(pe, 0, 0, OUT_REST)

        def lru_act(act):
            def block(j, par, last=False):
                def high(k0, k1):
                    if last:
                        to_high(act, 0, k0, k1)
                b = 2 * j + par
                su, sg = Strip(S_LRU, 2 * par, j, 4), Strip(S_LRU, 2 * par + 1, j, 4)
                act.wait_ge(S["strip_done"], su.s + 1)
                ge(act, L["xc_ready"], b)
                act.activation(upad[:, :, 2:2 + T], two(psum[:, U_BANK, :]), ACT.Copy).then_inc(L["u_evac"], 1)
                next_strip(split_hi, act, su)
                act.wait_ge(S["strip_done"], sg.s + 1)
                ge(act, L["lru_y"], b)
                act.activation(lw["sg"], psum[:, G_BANK, :], ACT.Tanh, scale=0.5).then_inc(L["tg_done"], 1)
                next_strip(split_hi, act, sg)
                mod_rows(act, M_LRU + b)
                ge(act, L["scan_done"], 4 * b)
                for d in range(2):
                    for g, dst in enumerate((lw["tr"][d], lw["ti"][d])):
                        act.wait_ge(L["gate_done"], 4 * b + 2 * d + g + 1)
                        act.activation(dst, psum[:, GATE_BANK + 2 * d + g, :], ACT.Tanh, scale=0.5,
                                       bias=half_gb[:, bass.ds(4 * b + 2 * d + g, 1)]).then_inc(L["gates_tanh"], 1)
                act.wait_ge(L["gates_tanh"], 4 * b + 4)
                for d in range(2):
                    high(2 * d, 2 * d + 2)
                    act.activation(lw["a"][d], lw["tr"][d], ACT.Exp, scale=neg_sp4[:, bass.ds(2 * b + d, 1)],
                                   bias=neg_sp4[:, bass.ds(2 * b + d, 1)])
                    act.activation(lw["th"][d], lw["tr"][d], ACT.Tanh, scale=sp4[:, bass.ds(2 * b + d, 1)],
                                   bias=sp4[:, bass.ds(2 * b + d, 1)]).then_inc(L["coef_step"], 1)
                for d in range(2):
                    act.wait_ge(L["coef_step"], 2 * b + d + 1)
                    act.activation(lw["tr"][d], lw["a"][d], ACT.Square).then_inc(L["coef_done"], 1)
                high(4, 10)
                for d in range(2):
                    act.wait_ge(L["m_done"], 2 * b + d + 1)
                    act.activation(lw["th"][d], lw["th"][d], ACT.Sqrt, scale=0.25).then_inc(L["sqrt_done"], 1)
                high(10, OUT_REST)
            block(0, 0)
            block(0, 1)
            with act.Fori(1, BLOCKS // 2 - 1) as j:
                for par in range(2):
                    block(j, par)
            for par in range(2):
                block(BLOCKS // 2 - 1, par, par == 1)

        def lru_dve(dve):
            dve.memset(upad[:, :, 0:2], 0.0)
            dve.memset(upad[:, :, 2 + T:], 0.0).then_inc(S["pads_zero"], 1)
            dve.wait_ge(S["pads_zero"], 1)

            def block(j, par, last=False):
                def low(k0, k1):
                    if last:
                        to_low(dve, 0, k0, k1)
                b = 2 * j + par
                su, sg = Strip(S_LRU, 2 * par, j, 4), Strip(S_LRU, 2 * par + 1, j, 4)
                dve.wait_ge(L["u_evac"], b + 1)
                if not (isinstance(b, int) and b == 0):
                    dve.wait_ge(L["gate_done"], 4 * b)
                xc = two(lw["xc"])
                step = Chain(dve, L["conv_step"], 3 * b, 3)
                step(dve.tensor_scalar(xc, upad[:, :, 0:T], col("conv_w", 4 * b), col("conv_b", b), ALU.mult, ALU.add))
                for w in range(1, CONV_W):
                    ins_ = dve.scalar_tensor_tensor(out=xc, in0=upad[:, :, w:w + T], scalar=col("conv_w", 4 * b + w),
                                                    in1=xc, op0=ALU.mult, op1=ALU.add)
                    if w < CONV_W - 1:
                        step(ins_)
                ins_.then_inc(L["xc_ready"], 1)
                step.close()
                next_strip(split_lo, dve, su)
                dve.wait_ge(L["tg_done"], b + 1)
                dve.scalar_tensor_tensor(out=lw["sg"], in0=lw["sg"], scalar=1.0, in1=psum[:, G_BANK, :],
                                         op0=ALU.add, op1=ALU.mult).then_inc(L["silu_done"], 1)
                next_strip(split_lo, dve, sg)
                mod_add(dve, M_LRU + b)
                low(0, 4)
                for d in range(2):
                    dve.wait_ge(L["coef_done"], 2 * b + d + 1)
                    dve.scalar_tensor_tensor(out=lw["th"][d], in0=lw["tr"][d], scalar=1.0, in1=lw["th"][d],
                                             op0=ALU.add, op1=ALU.mult).then_inc(L["m_done"], 1)
                dve.wait_ge(L["xc_ready"], b + 1)
                for d in range(2):
                    dve.scalar_tensor_tensor(out=lw["ti"][d], in0=lw["ti"][d], scalar=1.0, in1=lw["xc"],
                                             op0=ALU.add, op1=ALU.mult).then_inc(L["bx_done"], 1)
                low(4, 7)
                for d in range(2):
                    dve.wait_ge(L["sqrt_done"], 2 * b + d + 1)
                    dve.wait_ge(L["bx_done"], 2 * b + d + 1)
                    dve.tensor_tensor(lw["ti"][d], lw["ti"][d], lw["th"][d], ALU.mult).then_inc(L["b_done"], 1)
                low(7, 9)
                dve.wait_ge(L["m_done"], 2 * b + 2)
                hs = lw["tr"]
                for d, (a, bb) in enumerate(((slice(T, NT), NT - 1), (slice(NT - 1, T - 1, -1), T))):
                    dve.wait_ge(L["b_done"], 2 * b + d + 1)
                    dve.tensor_tensor_scan(hs[d][:, a], lw["a"][d][:, a], lw["ti"][d][:, a], 0.0, ALU.mult, ALU.add).then_inc(L["scan_done"], 1)
                for d, (a, bb) in enumerate(((slice(0, T), NT - 1), (slice(T - 1, None, -1), T))):
                    dve.wait_ge(L["scan_done"], 4 * b + d + 1)
                    dve.tensor_tensor_scan(hs[d][:, a], lw["a"][d][:, a], lw["ti"][d][:, a], hs[d][:, bb:bb + 1],
                                           ALU.mult, ALU.add).then_inc(L["scan_done"], 1)
                low(9, 12)
                dve.wait_ge(L["scan_done"], 4 * b + 4)
                dve.tensor_tensor(lw["a"][0], hs[0], hs[1], ALU.add).then_inc(L["ysum_done"], 1)
                dve.wait_ge(L["ysum_done"], b + 1)
                dve.wait_ge(L["silu_done"], b + 1)
                dve.scalar_tensor_tensor(out=y[:, :, b, :], in0=two(lw["a"][0]), scalar=0.5, in1=two(lw["sg"]),
                                         op0=ALU.mult, op1=ALU.mult).then_inc(L["lru_y"], 1)
                low(12, OUT_REST)
            block(0, 0)
            block(0, 1)
            with dve.Fori(1, BLOCKS // 2 - 1) as j:
                for par in range(2):
                    block(j, par)
            for par in range(2):
                block(BLOCKS // 2 - 1, par, par == 1)

        def rounds(eng, body, n, lag, peel=2):
            for i in range(peel):
                body(i // 2, i % 2)
            with eng.Fori(peel // 2, n // 2) as j:
                for par in range(2):
                    body(j, par)
            for i in range(n, n + lag):
                body(i // 2, i % 2)

        def live(i, n):
            return not isinstance(i, int) or 0 <= i < n

        asp = Space(yc_all, work_all)
        ksb, ksq, kr, vt_sb, v_sb = (asp(NT) for _ in range(5))
        p1 = [[asp(NT) for _ in range(2)] for _ in range(2)]
        attn1_t = asp(4 * T).rearrange("p (k q) -> p k q", k=4)
        qsb, qsq, qr, rtmp, osb, osq = (asp(T) for _ in range(6))
        sg1 = [asp(T), asp(T)]
        mx1, nm1, rs1 = tiny(4), tiny(4), tiny(4)
        K_BANK, Q_BANK, S_BANK, R_BANK, V_BANK, O_BANK, M_BANK = 0, 1, 2, 4, 4, 5, 6

        def att_strip(j, par, c):
            return Strip(S_ATT, 4 * par + c, j, 8)

        def att_pool(pool):
            with pool.Fori(0, HEADS1) as i:
                for q in range(4):
                    mod_load(pool, M_ATT + i, q)

        def att_pe(pe):
            def body(j, par):
                i = 2 * j + par
                here, before, older = live(i, HEADS1), live(i - 1, HEADS1), live(i - 2, HEADS1)

                def chunk(q):
                    return lambda half: mod_chunk(pe, M_ATT + i, q) if half else None
                first = isinstance(i, int) and i == 0
                last, end = (isinstance(i, int) and i == HEADS1 + n for n in range(2))
                if here:
                    ge(pe, A["v_evac"], i)
                    strip(pe, att_strip(j, par, 0), psum[:, K_BANK, :], NT, chunk(0),
                          operand=(S["h_ready"], KT) if first else None)
                if before:
                    pe.wait_ge(A["qr"], i)
                    pe.wait_ge(A["kr"], i)
                    ge(pe, A["attn_sb"], 2 * (i - 1))
                    pe.wait_ge(A["v_sb"], i)
                    ge(pe, A["o_evac"], i - 1)
                    for qt in range(2):
                        for c in range(2):
                            rows = slice(HD1 * c, HD1 * c + HD1)
                            mm = pe.matmul(psum[:, S_BANK + 2 * qt + c, :], qr[rows, qt * P:(qt + 1) * P], kr[rows, :],
                                           start=True, stop=True)
                        mm.then_inc(A["scores"], 1)
                if older:
                    pe.wait_ge(A["o_evac"], i - 1)
                    pe.matmul(psum[:, M_BANK, 0:T], ones, osq, start=True, stop=True).then_inc(A["sso"], 1)
                if here:
                    ge(pe, A["sgl"], i)
                    strip(pe, att_strip(j, par, 1), psum[:, Q_BANK, 0:T], T, chunk(1))
                    pe.wait_ge(A["k_evac"], i + 1)
                    if older:
                        pe.wait_ge(A["sdo"], i - 1)
                    if before:
                        pe.wait_ge(A["qr"], i)
                    pe.matmul(psum[:, M_BANK, :], ones64, ksq, start=True, stop=True).then_inc(A["ssk"], 1)
                    strip(pe, att_strip(j, par, 2), psum[:, K_BANK, :], NT, chunk(2))
                    pe.wait_ge(A["q_evac"], i + 1)
                    pe.wait_ge(A["sdk"], i + 1)
                    pe.matmul(psum[:, M_BANK, 0:T], ones64, qsq, start=True, stop=True).then_inc(A["ssq"], 1)
                    pe.wait_ge(A["kn"], i + 1)
                    ge(pe, A["expd"], 4 * i)
                    pe.matmul(psum[:, R_BANK, 0:T], rot1, ksb[:, 0:T], start=True, stop=True).then_inc(A["rotk"], 1)
                if last:
                    pe.wait_ge(A["v_evac"], HEADS1)
                    pe.wait_ge(A["sgl"], HEADS1)
                    out_first(pe, 1, 0, 6)
                if before:
                    for qt in range(2):
                        pe.wait_ge(A["attn"], 2 * (i - 1) + qt + 1)
                        for kt in range(4):
                            mm = pe.transpose(psum[:, S_BANK + qt, kt * P:(kt + 1) * P], p1[qt][0][:, kt * P:(kt + 1) * P], ident)
                        mm.then_inc(A["attn_t"], 1)
                if here:
                    strip(pe, att_strip(j, par, 3), psum[:, Q_BANK, 0:T], T, chunk(3))
                    pe.wait_ge(A["qn"], i + 1)
                    pe.wait_ge(A["sdq"], i + 1)
                    pe.matmul(psum[:, M_BANK, 0:T], rot1, qsb, start=True, stop=True).then_inc(A["rotq"], 1)
                if last:
                    out_first(pe, 1, 6, 10)
                if before:
                    pe.wait_ge(A["attn_sb"], 2 * i)
                    pe.wait_ge(A["v_sb"], i)
                    for kt in range(4):
                        mm = pe.matmul(psum[:, O_BANK, 0:T], v_sb[:, kt * P:(kt + 1) * P], attn1_t[:, kt, :],
                                       start=(kt == 0), stop=(kt == 3))
                    mm.then_inc(A["av"], 1)
                if last:
                    out_first(pe, 1, 10, 13)
                if end:
                    out_first(pe, 1, 13, OUT_REST)
                if here:
                    pe.wait_ge(A["v_evac"], i + 1)
                    pe.wait_ge(A["kt1"], i + 1)
                    for t in range(4):
                        mm = pe.transpose(psum[:, V_BANK, t * P:(t + 1) * P], vt_sb[:, t * P:(t + 1) * P], ident)
                    mm.then_inc(A["v_t"], 1)
                    mod_turn(pe, M_ATT + i, 1)
            rounds(pe, body, HEADS1, 2)

        def att_act(act):
            def body(j, par):
                i = 2 * j + par
                here, before, older = live(i, HEADS1), live(i - 1, HEADS1), live(i - 2, HEADS1)
                last = isinstance(i, int) and i == HEADS1
                if last:
                    to_high(act, 1, 0, 6)
                if here:
                    st = att_strip(j, par, 0)
                    act.wait_ge(S["strip_done"], st.s + 1)
                    ge(act, A["kr"], i)
                    act.activation(ksb, psum[:, K_BANK, :], ACT.Copy)
                    act.activation(ksq, psum[:, K_BANK, :], ACT.Square).then_inc(A["k_evac"], 1)
                    next_strip(split_hi, act, st)
                if before:
                    ge(act, A["attn_t"], 2 * (i - 1))
                    for qt in range(2):
                        act.wait_ge(A["negmax"], 2 * (i - 1) + qt + 1)
                        for c in range(2):
                            n = 2 * qt + c
                            act.activation(p1[qt][c], psum[:, S_BANK + n, :], ACT.Exp, bias=nm1[:, n:n + 1],
                                           accum_out=rs1[:, n:n + 1]).then_inc(A["expd"], 1)
                if older:
                    act.wait_ge(A["sso"], i - 1)
                    act.activation(osq, psum[:, M_BANK, 0:T], ACT.Sqrt, scale=1.0 / P, bias=eps_col).then_inc(A["sdo"], 1)
                if here:
                    st = att_strip(j, par, 1)
                    act.wait_ge(S["strip_done"], st.s + 1)
                    ge(act, A["qr"], i)
                    act.activation(qsb, psum[:, Q_BANK, 0:T], ACT.Copy)
                    act.activation(qsq, psum[:, Q_BANK, 0:T], ACT.Square).then_inc(A["q_evac"], 1)
                    next_strip(split_hi, act, st)
                    act.wait_ge(A["ssk"], i + 1)
                    act.activation(ksq, psum[:, M_BANK, :], ACT.Sqrt, scale=1.0 / HD1, bias=eps_col).then_inc(A["sdk"], 1)
                    st = att_strip(j, par, 2)
                    act.wait_ge(S["strip_done"], st.s + 1)
                    ge(act, A["v_t"], i)
                    act.activation(vt_sb, psum[:, K_BANK, :], ACT.Copy).then_inc(A["v_evac"], 1)
                    next_strip(split_hi, act, st)
                    act.wait_ge(A["ssq"], i + 1)
                    act.activation(qsq, psum[:, M_BANK, 0:T], ACT.Sqrt, scale=1.0 / HD1, bias=eps_col).then_inc(A["sdq"], 1)
                if last:
                    to_high(act, 1, 6, 10)
                if before:
                    ge(act, A["av"], i - 1)
                    for qt in range(2):
                        act.wait_ge(A["attn_t"], 2 * (i - 1) + qt + 1)
                        act.activation(attn1_t[:, :, qt * P:(qt + 1) * P],
                                       psum[:, S_BANK + qt, :].rearrange("p (k q) -> p k q", k=4), ACT.Copy).then_inc(A["attn_sb"], 1)
                if here:
                    st = att_strip(j, par, 3)
                    act.wait_ge(S["strip_done"], st.s + 1)
                    ge(act, A["att_y"], i - 1)
                    act.activation(sg1[par], psum[:, Q_BANK, 0:T], ACT.Tanh, scale=0.5).then_inc(A["tg"], 1)
                    next_strip(split_hi, act, st)
                    mod_rows(act, M_ATT + i)
                if last:
                    to_high(act, 1, 10, 13)
                if before:
                    act.wait_ge(A["av"], i)
                    ge(act, A["att_y"], i - 1)
                    act.activation(osb, psum[:, O_BANK, 0:T], ACT.Copy)
                    act.activation(osq, psum[:, O_BANK, 0:T], ACT.Square).then_inc(A["o_evac"], 1)
                if last:
                    to_high(act, 1, 13, OUT_REST)
                if here:
                    act.wait_ge(A["v_t"], i + 1)
                    ge(act, A["av"], i)
                    act.activation(v_sb, psum[:, V_BANK, :], ACT.Copy).then_inc(A["v_sb"], 1)
            rounds(act, body, HEADS1, 2)

        def att_dve(dve):
            kg = col("qk1", 1)

            def body(j, par):
                i = 2 * j + par
                here, before, older = live(i, HEADS1), live(i - 1, HEADS1), live(i - 2, HEADS1)
                last = isinstance(i, int) and i == HEADS1
                if last:
                    to_low(dve, 1, 0, 6)
                if here:
                    next_strip(split_lo, dve, att_strip(j, par, 0))
                if before:
                    for qt in range(2):
                        two_c = slice(2 * qt, 2 * qt + 2)
                        dve.wait_ge(A["scores"], 2 * (i - 1) + qt + 1)
                        dve.tensor_reduce(mx1[:, two_c], psum[:, S_BANK + 2 * qt:S_BANK + 2 * qt + 2, :], AX_X, ALU.max).then_inc(A["smax"], 1)
                        dve.wait_ge(A["smax"], 2 * (i - 1) + qt + 1)
                        dve.tensor_scalar(nm1[:, two_c], mx1[:, two_c], -1.0, None, ALU.mult).then_inc(A["negmax"], 1)
                if older:
                    dve.wait_ge(A["sdo"], i - 1)
                    dve.reciprocal(osq, osq).then_inc(A["rso"], 1)
                    dve.wait_ge(A["rso"], i - 1)
                    dve.scalar_tensor_tensor(out=osb, in0=osb, scalar=subg, in1=osq, op0=ALU.mult, op1=ALU.mult).then_inc(A["on"], 1)
                    dve.wait_ge(A["on"], i - 1)
                    dve.tensor_tensor(y[:, 0, i - 2, :], osb, sg1[par], ALU.mult).then_inc(A["att_y"], 1)
                if before:
                    for qt in range(2):
                        dve.wait_ge(A["expd"], 4 * (i - 1) + 2 * qt + 2)
                        dve.reciprocal(rs1[:, 2 * qt:2 * qt + 2], rs1[:, 2 * qt:2 * qt + 2]).then_inc(A["rsum"], 1)
                        dve.wait_ge(A["rsum"], 2 * (i - 1) + qt + 1)
                        dve.tensor_scalar(p1[qt][1], p1[qt][1], rs1[:, 2 * qt + 1:2 * qt + 2], lam_col, ALU.mult, ALU.mult).then_inc(A["p1s"], 1)
                        dve.wait_ge(A["p1s"], 2 * (i - 1) + qt + 1)
                        dve.scalar_tensor_tensor(out=p1[qt][0], in0=p1[qt][0], scalar=rs1[:, 2 * qt:2 * qt + 1], in1=p1[qt][1],
                                                 op0=ALU.mult, op1=ALU.subtract).then_inc(A["attn"], 1)
                if last:
                    to_low(dve, 1, 6, OUT_REST)
                if here:
                    next_strip(split_lo, dve, att_strip(j, par, 1))
                    dve.wait_ge(A["sdk"], i + 1)
                    dve.reciprocal(ksq, ksq).then_inc(A["rsk"], 1)
                    dve.wait_ge(A["rsk"], i + 1)
                    dve.scalar_tensor_tensor(out=kr[:, T:NT], in0=ksb[:, T:NT], scalar=kg, in1=ksq[:, T:NT], op0=ALU.mult, op1=ALU.mult)
                    dve.scalar_tensor_tensor(out=ksb[:, 0:T], in0=ksb[:, 0:T], scalar=kg, in1=ksq[:, 0:T], op0=ALU.mult, op1=ALU.mult).then_inc(A["kn"], 1)
                    next_strip(split_lo, dve, att_strip(j, par, 2))
                    dve.wait_ge(A["kn"], i + 1)
                    dve.tensor_tensor(kr[:, 0:T], ksb[:, 0:T], cos1, ALU.mult)
                    dve.wait_ge(A["rotk"], i + 1)
                    if before:
                        dve.wait_ge(A["qr"], i)
                    dve.tensor_tensor(rtmp, psum[:, R_BANK, 0:T], sin1, ALU.mult).then_inc(A["kt1"], 1)
                    dve.wait_ge(A["kt1"], i + 1)
                    dve.tensor_tensor(kr[:, 0:T], kr[:, 0:T], rtmp, ALU.add).then_inc(A["kr"], 1)
                    dve.wait_ge(A["sdq"], i + 1)
                    dve.reciprocal(qsq, qsq).then_inc(A["rsq"], 1)
                    dve.wait_ge(A["rsq"], i + 1)
                    dve.scalar_tensor_tensor(out=qsb, in0=qsb, scalar=qg1, in1=qsq, op0=ALU.mult, op1=ALU.mult).then_inc(A["qn"], 1)
                    next_strip(split_lo, dve, att_strip(j, par, 3))
                    dve.wait_ge(A["tg"], i + 1)
                    dve.scalar_tensor_tensor(out=sg1[par], in0=sg1[par], scalar=1.0, in1=psum[:, Q_BANK, 0:T],
                                             op0=ALU.add, op1=ALU.mult).then_inc(A["sgl"], 1)
                    dve.wait_ge(A["qn"], i + 1)
                    dve.wait_ge(A["kr"], i + 1)
                    dve.tensor_tensor(qr, qsb, cos1, ALU.mult)
                    dve.wait_ge(A["rotq"], i + 1)
                    dve.tensor_tensor(rtmp, psum[:, M_BANK, 0:T], sin1, ALU.mult).then_inc(A["qt1"], 1)
                    dve.wait_ge(A["qt1"], i + 1)
                    dve.tensor_tensor(qr, qr, rtmp, ALU.add).then_inc(A["qr"], 1)
                    mod_add(dve, M_ATT + i)
            rounds(dve, body, HEADS1, 2)

        gsp = Space(work_all)
        gu = [gsp(NT), gsp(NT)]
        gv, sz2, sqv, vn, gtmp = (gsp(NT) for _ in range(5))
        tabs = [gsp(2 * P), gsp(2 * P)]
        ssv = tiny(4)
        GU_BANK, GV_BANK, GZ_BANK, GT_BANK, GS_BANK = range(5)

        def sgu_strip(lay, j, par, c):
            return Strip(S_NET2 + lay * L2_STRIPS, 3 * par + c, j, 6)

        def sgu_pool(pool, lay):
            base = GROUPS * lay
            mods = lay == 0

            def table(g, par, first):
                if not first:
                    pool.wait_ge(G["gu_y"], base + g - 1)
                pool.dma_start(tabs[par], ins["sgu_tab"][base + g]).then_inc([G["tab_in0"], G["tab_in1"]][par], 16)
            if mods:
                for q in range(2):
                    mod_load(pool, M_SGU, q)
            pool.wait_ge(S["h_ready"], KT * (3 + lay))
            for par in range(2):
                table(par, par, True)
            def mod_group(g, ahead=0):
                if mods:
                    for q in range(ahead, 4):
                        mod_load(pool, M_SGU + g, q)
            mod_group(0, 2)
            with pool.Fori(0, GROUPS // 2 - 1) as j:
                for par in range(2):
                    mod_group(2 * j + par + 1)
                    table(2 * j + 2 + par, par, False)
            mod_group(GROUPS - 1)

        def sgu_pe(pe, lay):
            base, n, mods = GROUPS * lay, NT if lay == 0 else T, lay == 0
            nt = n // P

            def body(j, par):
                i = 2 * j + par
                here, before = live(i, GROUPS), live(i - 1, GROUPS)

                def chunk(q):
                    return lambda half: mod_chunk(pe, M_SGU + i, q) if half and mods else None
                if here:
                    ge(pe, G["gu"], base + i)
                    strip(pe, sgu_strip(lay, j, par, 0), psum[:, GU_BANK, 0:n], n, chunk(0),
                          operand=(S["h_ready"], KT * (2 + lay)) if isinstance(i, int) and i == 0 else None)
                if not here:
                    pe.wait_ge(G["gu"], GROUPS * (lay + 1))
                    pe.wait_ge(G["gv"], GROUPS * (lay + 1))
                    strip(pe, Strip(S_NET2 + lay * L2_STRIPS + L2_KV, 0), psum[:, 0, :], NT)
                if before:
                    pe.wait_ge(G["vn"], base + i)
                    tab = tabs[1 - par]
                    pe.wait_ge([G["tab_in0"], G["tab_in1"]][1 - par], 16 * (base // 2 + (j if par else j - 1) + 1))
                    ge(pe, G["sb1"], base + i - 1)
                    for t in range(nt):
                        mm = pe.matmul(psum[:, GS_BANK, t * P:(t + 1) * P], vn[:, t * P:(t + 1) * P], tab[:, 0:P],
                                       start=True, stop=True)
                    mm.then_inc(G["s"], 1)
                if here:
                    ge(pe, G["gv"], base + i)
                    strip(pe, sgu_strip(lay, j, par, 1), psum[:, GV_BANK, 0:n], n, chunk(1))
                    ge(pe, G["sz"], base + i)
                    strip(pe, sgu_strip(lay, j, par, 2), psum[:, GZ_BANK, 0:n], n, chunk(2))
                    pe.wait_ge(G["gv"], base + i + 1)
                    ge(pe, G["vn"], base + i)
                    for t in range(nt):
                        mm = pe.transpose(psum[:, GT_BANK, t * P:(t + 1) * P], gv[:, t * P:(t + 1) * P], ident)
                    mm.then_inc(G["v_t"], 1)
                    if mods:
                        mod_chunk(pe, M_SGU + i, 3)
                        mod_turn(pe, M_SGU + i, 1)
            rounds(pe, body, GROUPS, 1)

        def sgu_act(act, lay):
            base, n, mods = GROUPS * lay, NT if lay == 0 else T, lay == 0
            nt = n // P

            def body(j, par):
                i = 2 * j + par
                if not live(i, GROUPS):
                    return
                st = sgu_strip(lay, j, par, 0)
                act.wait_ge(S["strip_done"], st.s + 1)
                ge(act, G["gu_y"], base + i - 1)
                act.activation(gu[par][:, 0:n], psum[:, GU_BANK, 0:n], ACT.Gelu_apprx_tanh).then_inc(G["gu"], 1)
                next_strip(split_hi, act, st)
                st = sgu_strip(lay, j, par, 1)
                act.wait_ge(S["strip_done"], st.s + 1)
                ge(act, G["v_t"], base + i)
                act.activation(gv[:, 0:n], psum[:, GV_BANK, 0:n], ACT.Gelu_apprx_tanh).then_inc(G["gv"], 1)
                next_strip(split_hi, act, st)
                st = sgu_strip(lay, j, par, 2)
                act.wait_ge(S["strip_done"], st.s + 1)
                ge(act, G["gu_y"], base + i)
                act.activation(sz2[:, 0:n], psum[:, GZ_BANK, 0:n], ACT.Tanh, scale=0.5).then_inc(G["tz"], 1)
                next_strip(split_hi, act, st)
                act.wait_ge(G["v_t"], base + i + 1)
                ge(act, G["ssv"], base + i)
                act.activation(sqv[:, 0:n], psum[:, GT_BANK, 0:n], ACT.Square).then_inc(G["sqv"], 1)
                if mods:
                    mod_rows(act, M_SGU + i)
                act.wait_ge(G["ssv"], base + i + 1)
                act.activation(ssv[:, 0:nt], ssv[:, 0:nt], ACT.Sqrt, scale=1.0 / P, bias=eps_col).then_inc(G["sdv"], 1)
            rounds(act, body, GROUPS, 1)

        def sgu_dve(dve, lay):
            base, n, mods = GROUPS * lay, NT if lay == 0 else T, lay == 0
            nt = n // P

            def tiles(ap):
                return ap[:, 0:n].rearrange("p (t d) -> p t d", d=P)

            def body(j, par):
                i = 2 * j + par
                here, before = live(i, GROUPS), live(i - 1, GROUPS)
                if here:
                    next_strip(split_lo, dve, sgu_strip(lay, j, par, 0))
                if before:
                    tab = tabs[1 - par]
                    dve.wait_ge(G["s"], base + i)
                    dve.scalar_tensor_tensor(out=tiles(gtmp), in0=tiles(psum[:, GS_BANK, :]), scalar=col("v_norm", base + i - 1),
                                             in1=tab[:, P:2 * P].unsqueeze(1).to_broadcast([P, nt, P]),
                                             op0=ALU.mult, op1=ALU.add).then_inc(G["sb1"], 1)
                    dve.wait_ge(G["sb1"], base + i)
                    dve.tensor_tensor(gtmp[:, 0:n], gtmp[:, 0:n], gu[1 - par][:, 0:n], ALU.mult).then_inc(G["sb2"], 1)
                    dve.wait_ge(G["sb2"], base + i)
                    if lay == 0:
                        dve.scalar_tensor_tensor(out=y[:, :, i - 1, :], in0=two(gtmp), scalar=0.5, in1=two(sz2),
                                                 op0=ALU.mult, op1=ALU.mult).then_inc(G["gu_y"], 1)
                    else:
                        dve.scalar_tensor_tensor(out=y[:, 0, i - 1, :], in0=gtmp[:, 0:n], scalar=0.5, in1=sz2[:, 0:n],
                                                 op0=ALU.mult, op1=ALU.mult).then_inc(G["gu_y"], 1)
                if here:
                    next_strip(split_lo, dve, sgu_strip(lay, j, par, 1))
                    dve.wait_ge(G["tz"], base + i + 1)
                    dve.scalar_tensor_tensor(out=sz2[:, 0:n], in0=sz2[:, 0:n], scalar=1.0, in1=psum[:, GZ_BANK, 0:n],
                                             op0=ALU.add, op1=ALU.mult).then_inc(G["sz"], 1)
                    next_strip(split_lo, dve, sgu_strip(lay, j, par, 2))
                    dve.wait_ge(G["sqv"], base + i + 1)
                    dve.tensor_reduce(ssv[:, 0:nt], tiles(sqv), AX_X, ALU.add).then_inc(G["ssv"], 1)
                    if mods:
                        mod_add(dve, M_SGU + i)
                    dve.wait_ge(G["sdv"], base + i + 1)
                    dve.reciprocal(ssv[:, 0:nt], ssv[:, 0:nt]).then_inc(G["rsv"], 1)
                    dve.wait_ge(G["rsv"], base + i + 1)
                    ge(dve, G["s"], base + i)
                    for t in range(nt):
                        ins_ = dve.tensor_scalar(vn[:, t * P:(t + 1) * P], psum[:, GT_BANK, t * P:(t + 1) * P], ssv[:, t:t + 1],
                                                 None, ALU.mult)
                    ins_.then_inc(G["vn"], 1)
            rounds(dve, body, GROUPS, 1)

        bsp = Space(modraw_all, work_all)
        k2 = [bsp(NT), bsp(NT)]
        v2 = [bsp(NT), bsp(NT)]
        q2, q2s, q2r = (bsp(NT) for _ in range(3))
        r2tmp = bsp(T)
        p2 = [bsp(NT), bsp(NT), bsp(NT)]
        at2 = bsp(4 * T).rearrange("p (k q) -> p k q", k=4)
        at2c = bsp(2 * T).rearrange("p (k q) -> p k q", k=2)
        sz3 = [bsp(NT), bsp(NT)]
        mx2, nm2, rs2 = tiny(4), tiny(4), tiny(4)
        kv_k, kv_sq, kv_v = p2[0:2], p2[2], [q2, q2r]

        def kv_strip(lay, c):
            return Strip(S_NET2 + lay * L2_STRIPS + L2_KV, c)

        def kv_pe(pe, lay):
            base = 2 * lay
            strip(pe, kv_strip(lay, 1), psum[:, 1, :], NT)
            for n in range(2):
                pe.wait_ge(B["k_evac"], base + n + 1)
                if n:
                    pe.wait_ge(B["sdk"], base + n)
                pe.matmul(psum[:, 6, :], ones, kv_sq, start=True, stop=True).then_inc(B["ssk"], 1)
                strip(pe, kv_strip(lay, 2 + n), psum[:, n, :], NT)
                pe.wait_ge(B["kn"], base + n + 1)
                if n:
                    pe.wait_ge(B["kt1"], base + n)
                pe.matmul(psum[:, 5, 0:T], rot2, kv_k[n][:, 0:T], start=True, stop=True).then_inc(B["rotk"], 1)
            pe.wait_ge(G["gu_y"], GROUPS * (lay + 1))
            if lay == 0:
                pe.wait_ge(S["mod_cols"], MOD_GROUPS)
            for n in range(2):
                pe.wait_ge(B["v_evac"], base + n + 1)
                for t in range(4):
                    mm = pe.transpose(psum[:, 3 + n, t * P:(t + 1) * P], kv_v[n][:, t * P:(t + 1) * P], ident)
                mm.then_inc(B["v_t"], 1)

        def kv_act(act, lay):
            base = 2 * lay
            act.wait_ge(G["gu_y"], GROUPS * (lay + 1))
            for n in range(2):
                st = kv_strip(lay, n)
                act.wait_ge(S["strip_done"], st.s + 1)
                act.activation(kv_k[n], psum[:, n, :], ACT.Copy)
                if n:
                    act.wait_ge(B["kn"], base + n)
                act.activation(kv_sq, psum[:, n, :], ACT.Square).then_inc(B["k_evac"], 1)
                next_strip(split_hi, act, st)
                act.wait_ge(B["ssk"], base + n + 1)
                act.activation(kv_sq, psum[:, 6, :], ACT.Sqrt, scale=1.0 / P, bias=eps_col).then_inc(B["sdk"], 1)
            for n in range(2):
                st = kv_strip(lay, 2 + n)
                act.wait_ge(S["strip_done"], st.s + 1)
                act.activation(kv_v[n], psum[:, n, :], ACT.Copy).then_inc(B["v_evac"], 1)
                next_strip(split_hi, act, st)
            for n in range(2):
                act.wait_ge(B["v_t"], base + n + 1)
                act.activation(v2[n], psum[:, 3 + n, :], ACT.Copy).then_inc(B["v_sb"], 1)

        def kv_dve(dve, lay):
            base = 2 * lay
            kg = col("qk2", 2 + lay)
            for n in range(2):
                next_strip(split_lo, dve, kv_strip(lay, n))
                dve.wait_ge(B["sdk"], base + n + 1)
                dve.reciprocal(kv_sq, kv_sq).then_inc(B["rsk"], 1)
                dve.wait_ge(B["rsk"], base + n + 1)
                dve.scalar_tensor_tensor(out=k2[n][:, T:NT], in0=kv_k[n][:, T:NT], scalar=kg, in1=kv_sq[:, T:NT], op0=ALU.mult, op1=ALU.mult)
                dve.scalar_tensor_tensor(out=kv_k[n][:, 0:T], in0=kv_k[n][:, 0:T], scalar=kg, in1=kv_sq[:, 0:T],
                                         op0=ALU.mult, op1=ALU.mult).then_inc(B["kn"], 1)
            for n in range(2):
                next_strip(split_lo, dve, kv_strip(lay, 2 + n))
                dve.wait_ge(B["kn"], base + n + 1)
                dve.tensor_tensor(k2[n][:, 0:T], kv_k[n][:, 0:T], cos2, ALU.mult)
                dve.wait_ge(B["rotk"], base + n + 1)
                if n:
                    dve.wait_ge(B["kr"], base + n)
                dve.tensor_tensor(r2tmp, psum[:, 5, 0:T], sin2, ALU.mult).then_inc(B["kt1"], 1)
                dve.wait_ge(B["kt1"], base + n + 1)
                dve.tensor_tensor(k2[n][:, 0:T], k2[n][:, 0:T], r2tmp, ALU.add).then_inc(B["kr"], 1)

        def gqa_strip(lay, j, par, c):
            return Strip(S_NET2 + lay * L2_STRIPS + L2_ATT, 2 * par + c, j, 4)

        def gqa_pe(pe, lay):
            base, wide_ = HEADS2 * lay, lay == 0
            n = NT if wide_ else T
            def body(j, par):
                i = 2 * j + par
                here, before, older = live(i, HEADS2), live(i - 1, HEADS2), live(i - 2, HEADS2)
                last, end = (isinstance(i, int) and i == HEADS2 + n for n in range(2))
                if last:
                    pe.wait_ge(B["q_evac"], base + HEADS2)
                    pe.wait_ge(B["sz"], base + HEADS2)
                    out_first(pe, 2 + lay, 0, 4)
                if end:
                    out_first(pe, 2 + lay, 10, 14)
                if here:
                    ge(pe, B["q_evac"], base + i)
                    strip(pe, gqa_strip(lay, j, par, 0), psum[:, 0, 0:n], n)
                if before:
                    pe.wait_ge(B["qn"], base + i)
                    ge(pe, B["qt1"], base + i - 1)
                    pe.matmul(psum[:, 5, 0:T], rot2, q2[:, 0:T], start=True, stop=True).then_inc(B["rotq"], 1)
                if last:
                    out_first(pe, 2 + lay, 4, 8)
                if older:
                    pe.wait_ge(B["attn"], base + i - 1)
                    for qt in range(2):
                        for kt in range(4):
                            mm = pe.transpose(psum[:, 2 + qt, kt * P:(kt + 1) * P], p2[qt][:, kt * P:(kt + 1) * P], ident)
                    if wide_:
                        for qt in range(2):
                            for kt in range(2):
                                mm = pe.transpose(psum[:, 4, kt * T + qt * P:kt * T + (qt + 1) * P],
                                                  p2[2][:, qt * T + kt * P:qt * T + (kt + 1) * P], ident)
                    mm.then_inc(B["attn_t"], 1)
                if here:
                    ge(pe, B["sz"], base + i)
                    strip(pe, gqa_strip(lay, j, par, 1), psum[:, 1, 0:n], n)
                    pe.wait_ge(B["q_evac"], base + i + 1)
                    ge(pe, B["sdq"], base + i)
                    pe.matmul(psum[:, 6, 0:n], ones, q2s[:, 0:n], start=True, stop=True).then_inc(B["ssq"], 1)
                if last:
                    out_first(pe, 2 + lay, 8, 10)
                if end:
                    out_first(pe, 2 + lay, 14, OUT_REST)
                if older:
                    pe.wait_ge(B["attn_sb"], base + i - 1)
                    ge(pe, B["y2"], base + i - 2)
                    for kt in range(4):
                        mm = pe.matmul(psum[:, 7, 0:T], v2[par][:, kt * P:(kt + 1) * P], at2[:, kt, :], start=(kt == 0), stop=(kt == 3))
                    if wide_:
                        for kt in range(2):
                            mm = pe.matmul(psum[:, 7, T:NT], v2[par][:, T + kt * P:T + (kt + 1) * P], at2c[:, kt, :],
                                           start=(kt == 0), stop=(kt == 1))
                    mm.then_inc(B["av"], 1)
                if before:
                    if isinstance(i, int) and i == 1:
                        pe.wait_ge(B["kr"], 2 * (lay + 1))
                        pe.wait_ge(B["v_sb"], 2 * (lay + 1))
                    pe.wait_ge(B["qr"], base + i)
                    ge(pe, B["attn_sb"], base + i - 1)
                    keys = k2[1 - par]
                    for qt in range(2):
                        mm = pe.matmul(psum[:, 2 + qt, :], q2r[:, qt * P:(qt + 1) * P], keys, start=True, stop=True)
                    if wide_:
                        for qt in range(2):
                            mm = pe.matmul(psum[:, 4, qt * T:(qt + 1) * T], q2r[:, T + qt * P:T + (qt + 1) * P], keys[:, T:NT],
                                           start=True, stop=True)
                    mm.then_inc(B["scores"], 1)
            rounds(pe, body, HEADS2, 2, 4)

        def gqa_act(act, lay):
            base, wide_ = HEADS2 * lay, lay == 0
            n = NT if wide_ else T

            def body(j, par):
                i = 2 * j + par
                here, before, older = live(i, HEADS2), live(i - 1, HEADS2), live(i - 2, HEADS2)
                last, end = (isinstance(i, int) and i == HEADS2 + n for n in range(2))
                if before:
                    act.wait_ge(B["ssq"], base + i)
                    act.activation(q2s[:, 0:n], psum[:, 6, 0:n], ACT.Sqrt, scale=1.0 / P, bias=eps_col).then_inc(B["sdq"], 1)
                if last:
                    to_high(act, 2 + lay, 0, 4)
                if older:
                    act.wait_ge(B["negmax"], base + i - 1)
                    ge(act, B["attn_t"], base + i - 2)
                    for qt in range(2):
                        ins_ = act.activation(p2[qt], psum[:, 2 + qt, :], ACT.Exp, scale=SCALE2, bias=nm2[:, qt:qt + 1],
                                              accum_out=rs2[:, qt:qt + 1])
                    if wide_:
                        for qt in range(2):
                            ins_ = act.activation(p2[2][:, qt * T:(qt + 1) * T], psum[:, 4, qt * T:(qt + 1) * T], ACT.Exp, scale=SCALE2,
                                                  bias=nm2[:, 2 + qt:3 + qt], accum_out=rs2[:, 2 + qt:3 + qt])
                    ins_.then_inc(B["expd"], 1)
                if last:
                    to_high(act, 2 + lay, 4, 8)
                if end:
                    to_high(act, 2 + lay, 14, OUT_REST)
                if here:
                    st = gqa_strip(lay, j, par, 0)
                    act.wait_ge(S["strip_done"], st.s + 1)
                    next_strip(split_hi, act, st)
                    ge(act, B["qr"], base + i)
                    if isinstance(i, int) and i == 0:
                        act.wait_ge(B["v_t"], 2 * (lay + 1))
                    act.activation(q2[:, 0:n], psum[:, 0, 0:n], ACT.Copy)
                    act.activation(q2s[:, 0:n], psum[:, 0, 0:n], ACT.Square).then_inc(B["q_evac"], 1)
                if older:
                    act.wait_ge(B["attn_t"], base + i - 1)
                    ge(act, B["av"], base + i - 2)
                    for qt in range(2):
                        ins_ = act.activation(at2[:, :, qt * P:(qt + 1) * P],
                                              psum[:, 2 + qt, :].rearrange("p (k q) -> p k q", k=4), ACT.Copy)
                    if wide_:
                        ins_ = act.activation(at2c, psum[:, 4, :].rearrange("p (k q) -> p k q", k=2), ACT.Copy)
                    ins_.then_inc(B["attn_sb"], 1)
                if last:
                    to_high(act, 2 + lay, 8, 14)
                if here:
                    st = gqa_strip(lay, j, par, 1)
                    act.wait_ge(S["strip_done"], st.s + 1)
                    next_strip(split_hi, act, st)
                    ge(act, B["y2"], base + i - 1)
                    act.activation(sz3[par][:, 0:n], psum[:, 1, 0:n], ACT.Tanh, scale=0.5).then_inc(B["tz"], 1)
            rounds(act, body, HEADS2, 2, 4)

        def gqa_dve(dve, lay):
            base, wide_ = HEADS2 * lay, lay == 0
            n = NT if wide_ else T
            nq = 4 if wide_ else 2
            qg = col("qk2", lay)

            def body(j, par):
                i = 2 * j + par
                here, before, older = live(i, HEADS2), live(i - 1, HEADS2), live(i - 2, HEADS2)
                last, end = (isinstance(i, int) and i == HEADS2 + n for n in range(2))
                if older:
                    dve.wait_ge(B["scores"], base + i - 1)
                    ins_ = dve.tensor_reduce(mx2[:, 0:2], psum[:, 2:4, :], AX_X, ALU.max)
                    if wide_:
                        ins_ = dve.tensor_reduce(mx2[:, 2:4], two(psum[:, 4, :]), AX_X, ALU.max)
                    ins_.then_inc(B["smax"], 1)
                    dve.wait_ge(B["smax"], base + i - 1)
                    dve.tensor_scalar(nm2[:, 0:nq], mx2[:, 0:nq], -SCALE2, None, ALU.mult).then_inc(B["negmax"], 1)
                if last:
                    to_low(dve, 2 + lay, 0, 4)
                if end:
                    to_low(dve, 2 + lay, 10, 14)
                if before:
                    dve.wait_ge(B["sdq"], base + i)
                    dve.reciprocal(q2s[:, 0:n], q2s[:, 0:n]).then_inc(B["rsq"], 1)
                    dve.wait_ge(B["rsq"], base + i)
                    ge(dve, B["scores"], base + i - 1)
                    if isinstance(i, int) and i == 1:
                        dve.wait_ge(B["v_t"], 2 * (lay + 1))
                    if wide_:
                        dve.scalar_tensor_tensor(out=q2r[:, T:NT], in0=q2[:, T:NT], scalar=qg, in1=q2s[:, T:NT], op0=ALU.mult, op1=ALU.mult)
                    dve.scalar_tensor_tensor(out=q2[:, 0:T], in0=q2[:, 0:T], scalar=qg, in1=q2s[:, 0:T], op0=ALU.mult, op1=ALU.mult).then_inc(B["qn"], 1)
                if older:
                    dve.wait_ge(B["expd"], base + i - 1)
                    dve.reciprocal(rs2[:, 0:nq], rs2[:, 0:nq]).then_inc(B["rsum"], 1)
                    dve.wait_ge(B["rsum"], base + i - 1)
                    for qt in range(2):
                        ins_ = dve.tensor_scalar(p2[qt], p2[qt], rs2[:, qt:qt + 1], None, ALU.mult)
                    if wide_:
                        for qt in range(2):
                            ins_ = dve.tensor_scalar(p2[2][:, qt * T:(qt + 1) * T], p2[2][:, qt * T:(qt + 1) * T], rs2[:, 2 + qt:3 + qt],
                                                     None, ALU.mult)
                    ins_.then_inc(B["attn"], 1)
                if last:
                    to_low(dve, 2 + lay, 4, 8)
                if end:
                    to_low(dve, 2 + lay, 14, OUT_REST)
                if here:
                    next_strip(split_lo, dve, gqa_strip(lay, j, par, 0))
                if before:
                    dve.wait_ge(B["qn"], base + i)
                    dve.tensor_tensor(q2r[:, 0:T], q2[:, 0:T], cos2, ALU.mult)
                    dve.wait_ge(B["rotq"], base + i)
                    ge(dve, B["qr"], base + i - 1)
                    dve.tensor_tensor(r2tmp, psum[:, 5, 0:T], sin2, ALU.mult).then_inc(B["qt1"], 1)
                    dve.wait_ge(B["qt1"], base + i)
                    dve.tensor_tensor(q2r[:, 0:T], q2r[:, 0:T], r2tmp, ALU.add).then_inc(B["qr"], 1)
                if last:
                    to_low(dve, 2 + lay, 8, 10)
                if here:
                    next_strip(split_lo, dve, gqa_strip(lay, j, par, 1))
                if older:
                    dve.wait_ge(B["av"], base + i - 1)
                    tile = GROUPS + i - 2
                    if wide_:
                        dve.scalar_tensor_tensor(out=y[:, :, tile, :], in0=two(psum[:, 7, :]), scalar=0.5, in1=two(sz3[par]),
                                                 op0=ALU.mult, op1=ALU.mult).then_inc(B["y2"], 1)
                    else:
                        dve.scalar_tensor_tensor(out=y[:, 0, tile, :], in0=psum[:, 7, 0:T], scalar=0.5, in1=sz3[par][:, 0:T],
                                                 op0=ALU.mult, op1=ALU.mult).then_inc(B["y2"], 1)
                if here:
                    dve.wait_ge(B["tz"], base + i + 1)
                    dve.scalar_tensor_tensor(out=sz3[par][:, 0:n], in0=sz3[par][:, 0:n], scalar=1.0, in1=psum[:, 1, 0:n],
                                             op0=ALU.add, op1=ALU.mult).then_inc(B["sz"], 1)
            rounds(dve, body, HEADS2, 2)

        zt = Space((work[:, 6 * NT:WORK], WORK - 6 * NT))
        ctan = zt(4 * KT)
        sp_n, sp_z, sp_w, sp_r = (zt(2 * BLOCKS) for _ in range(4))
        lam_p, lam_e = zt(2), zt(2)
        LOG1P = [1.0 / (2 * n + 1) for n in range(8, 0, -1)]

        y_slots = y[:, 0, :, :].rearrange("p k t -> p (k t)").rearrange("p (a j c) -> p a j c", a=2, j=4)
        first_slot = [modraw[:, 0, :, :], modraw[:, 1, :, :], y_slots[:, 0, :, :], y_slots[:, 1, :, :]]
        first_bank = [pmod, psum[:, 5, :]]

        def start_pool(pool):
            pool.memset(cond[:, :, :], 0.0).then_inc(S["start_tab"], 1)
            pool.memset(eps_col, EPS).then_inc(S["start_tab"], 1)

            def load(m, q, first):
                if not first:
                    pool.wait_ge(S["mod_used"], 4 * (m - 1) + q + 1)
                pool.dma_start(first_slot[q], ins["mod_weights"][4 * m + q]).then_inc(first_in[q], 16)
            for q in range(4):
                load(0, q, True)
            with pool.Fori(1, MOD_FIRST) as m:
                for q in range(4):
                    load(m, q, False)

        def start_act(act):
            act.wait_ge(S["cols_in"], 16)
            act.activation(ctan, col("c", 0, 4 * KT), ACT.Tanh, scale=0.5).then_inc(S["cond_tanh"], 1)
            act.wait_ge(S["start_dve"], 1)
            act.activation(sp_z, sp_z, ACT.Exp, scale=-1.0).then_inc(S["start_act"], 1)
            act.wait_ge(S["start_pe"], 1)
            act.activation(lam_e, psum[:, 0, 0:2], ACT.Exp).then_inc(S["start_act"], 1)
            act.wait_ge(S["x_in"], 32)

            def square(k, par, first):
                if not first:
                    act.wait_ge(S["sq_added"], k - 1)
                act.activation(sqb[par][:, 0:T], xl[:, k, :], ACT.Square)
                act.activation(sqb[par][:, T:NT], y[:, 1, k, :], ACT.Square).then_inc(S["sq_done"], 1)
            for par in range(2):
                square(par, par, True)
            with act.Fori(1, KT // 2) as j:
                for par in range(2):
                    square(2 * j + par, par, False)
            for c in range(2):
                split_hi(act, 0, c)
            act.wait_ge(S["start_tab"], 2)
            mod_rows(act, 0, first_bank[0])
            norm_sqrt(act, 0)

            def high(j):
                for c in range(4):
                    act.wait_ge(S["hf_done"], 4 * j + c + 1)
                    act.activation(h_hi[:, 4 * j + c, :], hs4[c], ACT.Copy).then_inc(S["hhi_done"], 1)
            mod_rows(act, 1, first_bank[1])
            high(0)
            with act.Fori(1, MOD_FIRST // 2) as j:
                for par in range(2):
                    mod_rows(act, 2 * j + par, first_bank[par])
                high(j)

        def start_dve(dve):
            n = [0]

            def step(ins_):
                n[0] += 1
                ins_.then_inc(S["start_dve"], 1)
                dve.wait_ge(S["start_dve"], n[0])
            dve.wait_ge(S["cols_in"], 16)
            lam = col("lam", 0, 2 * BLOCKS)
            dve.scalar_tensor_tensor(out=sp_z, in0=lam, scalar=-1.0, in1=lam, op0=ALU.mult, op1=ALU.max)
            dve.tensor_tensor(lam_p[:, 0:1], col("att_lam", 0), col("att_lam", 1), ALU.mult)
            dve.tensor_scalar(half_gb, col("gate_b", 0, 4 * BLOCKS), 0.5, None, ALU.mult)
            dve.tensor_scalar(qg1, col("qk1", 0), float(HD1) ** -0.5, None, ALU.mult)
            dve.tensor_scalar(subg, col("subln", 0), (1.0 - LAM_INIT) * 0.5, None, ALU.mult)
            dve.tensor_scalar(sp_n, lam, -1.0, 0.0, ALU.mult, ALU.max)
            step(dve.tensor_tensor(lam_p[:, 1:2], col("att_lam", 2), col("att_lam", 3), ALU.mult))
            dve.wait_ge(S["cond_tanh"], 1)
            step(dve.scalar_tensor_tensor(out=ctan, in0=ctan, scalar=1.0, in1=col("c", 0, 4 * KT), op0=ALU.add, op1=ALU.mult))
            dve.wait_ge(S["start_tab"], 1)
            dve.tensor_scalar(cond[:, :, 0:4].rearrange("p k v -> p v k"), ctan.rearrange("p (v k) -> p v k", v=4),
                              0.5, None, ALU.mult).then_inc(S["cond_ready"], 1)
            dve.wait_ge(S["start_act"], 1)
            step(dve.tensor_scalar(sp_w, sp_z, 2.0, None, ALU.add))
            step(dve.reciprocal(sp_w, sp_w))
            step(dve.tensor_tensor(sp_w, sp_w, sp_z, ALU.mult))
            step(dve.tensor_tensor(sp_z, sp_w, sp_w, ALU.mult))
            step(dve.tensor_scalar(sp_r, sp_z, LOG1P[0], None, ALU.mult))
            for c in LOG1P[1:]:
                step(dve.scalar_tensor_tensor(out=sp_r, in0=sp_r, scalar=c, in1=sp_z, op0=ALU.add, op1=ALU.mult))
            step(dve.scalar_tensor_tensor(out=sp_r, in0=sp_r, scalar=1.0, in1=sp_w, op0=ALU.add, op1=ALU.mult))
            step(dve.scalar_tensor_tensor(out=sp_r, in0=sp_r, scalar=2.0, in1=sp_n, op0=ALU.mult, op1=ALU.add))
            dve.tensor_scalar(sp4, sp_r, 4.0, None, ALU.mult)
            step(dve.tensor_scalar(neg_sp4, sp_r, -4.0, None, ALU.mult))
            dve.wait_ge(S["start_act"], 2)
            step(dve.tensor_tensor(lam_col, lam_e[:, 0:1], lam_e[:, 1:2], ALU.subtract))
            step(dve.tensor_scalar(lam_col, lam_col, LAM_INIT, None, ALU.add))
            def add(k, par):
                dve.wait_ge(S["sq_done"], k + 1)
                dve.wait_ge(S["sq_added"], k)
                dve.tensor_tensor(acc, acc, sqb[par], ALU.add).then_inc(S["sq_added"], 1)
            dve.wait_ge(S["sq_done"], 1)
            dve.tensor_copy(acc, sqb[0]).then_inc(S["sq_added"], 1)
            add(1, 1)
            with dve.Fori(1, KT // 2 - 1) as j:
                for par in range(2):
                    add(2 * j + par, par)
            for c in range(2):
                split_lo(dve, 0, c)
            mod_add(dve, 0, first_bank[0], 0)
            norm_reciprocal(dve, 0)
            dve.wait_ge(S["rstd_done"], 1)
            for x, s in ((xl[:, :, :], 0), (y[:, 1, :, :], 1)):
                dve.tensor_tensor(x, x, nb["rstd"][:, s * T:(s + 1) * T].unsqueeze(1).to_broadcast([P, KT, T]),
                                  ALU.mult).then_inc(S["xn_done"], 1)

            def modulate(j, first=False):
                ks = bass.ds(4 * j, 4)
                dve.wait_ge(S["mod_cols"], 2 * j + 2)
                dve.scalar_tensor_tensor(
                    out=mod_a[:, ks, :], in0=mod[:, bass.ds(16 + 4 * j, 4), :], scalar=1.0,
                    in1=col("norm_g", 4 * j, 4).unsqueeze(2).to_broadcast([P, 4, 2]),
                    op0=ALU.add, op1=ALU.mult).then_inc(S["mod_a_done"], 1)
                dve.wait_ge(S["mod_a_done"], j + 1)
                dve.wait_ge(S["xn_done"], 2)
                if not first:
                    dve.wait_ge(S["h_ready"], 4 * j)
                for c in range(4):
                    k = 4 * j + c
                    for s, x in enumerate((xl[:, bass.ds(k, 1), :], y[:, 1, bass.ds(k, 1), :])):
                        ins_ = dve.tensor_scalar(hs4[c][:, s * T:(s + 1) * T].unsqueeze(1), x, mod_a[:, bass.ds(k, 1), s],
                                                 mod[:, bass.ds(k, 1), s], ALU.mult, ALU.add)
                    ins_.then_inc(S["hf_done"], 1)
                for c in range(4):
                    k = 4 * j + c
                    dve.wait_ge(S["hhi_done"], k + 1)
                    dve.tensor_tensor(h_lo[:, k, :], hs4[c], h_hi[:, k, :].bitcast(F32), ALU.subtract).then_inc(S["h_ready"], 1)
            mod_add(dve, 1, first_bank[1], 4)
            modulate(0, True)
            with dve.Fori(1, MOD_FIRST // 2) as j:
                for par in range(2):
                    mod_add(dve, 2 * j + par, first_bank[par], j + 4 * par)
                modulate(j)

        def start_pe(pe):
            pe.wait_ge(S["consts_in"], 16)
            pe.wait_ge(S["start_dve"], 1)
            pe.matmul(psum[:, 0, 0:2], ones, lam_p, start=True, stop=True).then_inc(S["start_pe"], 1)
            pe.wait_ge(S["cond_ready"], 1)

            def products(m, par):
                if not (isinstance(m, int) and m < 2):
                    pe.wait_ge(S["mod_cols"], m - 1)
                for q in range(4):
                    pe.wait_ge(first_in[q], 16 * (m + 1))
                    mod_products(pe, first_bank[par], first_slot[q], q)
            products(0, 0)
            products(1, 1)
            mod_turn(pe, 0, 0, first_bank[0])
            norm_pe(pe, 0)
            with pe.Fori(1, MOD_FIRST // 2) as j:
                for par in range(2):
                    products(2 * j + par, par)
                    mod_turn(pe, 2 * j + par - 1, 0, first_bank[1 - par])
            mod_turn(pe, MOD_FIRST - 1, 0, first_bank[1])

        block = ctx.enter_context(nc.Block())

        @block.sync
        def _(sp):
            sp.dma_start(cols[:, :], ins["cols"]).then_inc(S["cols_in"], 16)
            sp.dma_start(consts[:, :], ins["consts"]).then_inc(S["consts_in"], 16)
            x_t = ins["x_t"].rearrange("k p t -> p k t")
            sp.dma_start(xl[:, :, :], x_t[:, :, 0:T]).then_inc(S["x_in"], 16)
            sp.dma_start(y[:, 1, :, :], x_t[:, :, T:NT]).then_inc(S["x_in"], 16)
            for par in range(2):
                load_strip(sp, 0, par, True)
            sp.wait_ge(S["mod_used"], 4 * (MOD_FIRST - 2))
            with sp.Fori(1, N_STRIPS // 2) as pair:
                for par in range(2):
                    load_strip(sp, pair, par)
            for k in range(0, KT, 2):
                sp.wait_ge(S["x_new"], 3 * KT + k + 2)
                sp.dma_start(out[k:k + 2].rearrange("k p t -> p k t"), xl[:, k:k + 2, :]).then_inc(S["out_stored"], 16)
            sp.wait_ge(S["out_stored"], 16 * KT // 2)

        @block.gpsimd
        def _(pool):
            start_pool(pool)
            lru_pool(pool)
            out_pool(pool, 0)
            norm_pool(pool, 1)
            att_pool(pool)
            pool.wait_ge(A["att_y"], HEADS1)
            pool.dma_start(y[:, 1, :, :], ins["ctx2_t"].rearrange("k p t -> p k t")).then_inc(S["ctx2_in"], 16)
            out_pool(pool, 1)
            for lay in range(2):
                norm_pool(pool, 2 + lay)
                sgu_pool(pool, lay)
                out_pool(pool, 2 + lay)

        @block.scalar
        def _(act):
            start_act(act)
            lru_act(act)
            out_act(act, 0)
            norm_act(act, 1)
            att_act(act)
            out_act(act, 1)
            for lay in range(2):
                norm_act(act, 2 + lay)
                sgu_act(act, lay)
                kv_act(act, lay)
                gqa_act(act, lay)
                out_act(act, 2 + lay)

        @block.vector
        def _(dve):
            start_dve(dve)
            lru_dve(dve)
            out_dve(dve, 0)
            norm_dve(dve, 1)
            att_dve(dve)
            out_dve(dve, 1)
            for lay in range(2):
                norm_dve(dve, 2 + lay)
                sgu_dve(dve, lay)
                kv_dve(dve, lay)
                gqa_dve(dve, lay)
                out_dve(dve, 2 + lay)

        @block.tensor
        def _(pe):
            start_pe(pe)
            lru_pe(pe)
            out_pe(pe, 0)
            norm_pe(pe, 1)
            att_pe(pe)
            out_pe(pe, 1)
            for lay in range(2):
                norm_pe(pe, 2 + lay)
                sgu_pe(pe, lay)
                kv_pe(pe, lay)
                gqa_pe(pe, lay)
                out_pe(pe, 2 + lay)


def _strips(w, columns, rows=range(KT)):
    tiles = w.reshape(KT, P, -1, P)[list(rows)][:, :, columns, :]
    tiles = tiles.reshape(2, HALF, P, len(columns), P).transpose(3, 0, 2, 1, 4)
    return np.ascontiguousarray(tiles).reshape(2 * len(columns), P, HALF * P)


def _stream(i):
    parts = [
        _strips(i["lru_w_in"][0], [c for b in range(BLOCKS) for c in (b, BLOCKS + b)]),
        _strips(i["lru_w_out"][0], list(range(KT))),
        _strips(i["att_w_in"][0], [c for h in range(HEADS1) for c in (HEADS1 + h, h, 2 * HEADS1 + h, 3 * HEADS1 + h)]),
        _strips(i["att_w_out"][0], list(range(KT))),
    ]
    u, v, z, q, k, zb = 0, 8, 16, 24, 32, 36
    heads = [kv * REP2 + r for r in range(REP2) for kv in range(KV2)]
    order = ([c for g in range(GROUPS) for c in (u + g, v + g, z + g)] + [k, k + 1, k + 2, k + 3]
             + [c for h in heads for c in (q + h, zb + h)])
    for lay in range(2):
        parts += [_strips(i["w_in_2"][lay], order), _strips(i["w_out_2"][lay], list(range(KT)), list(range(GROUPS)) + [GROUPS + h for h in heads])]
    return np.concatenate(parts)


def _mod_stream(i):
    w = np.concatenate([i["mod_w"], i["w_mod_2"]]).reshape(4, 4, 4, P, 12, 512)
    w = w.transpose(0, 4, 1, 3, 2, 5).reshape(MOD_GROUPS, 4, P, 4, 512)
    order = [m // 2 + MOD_FIRST // 2 * (m % 2) for m in range(MOD_FIRST)] + list(range(MOD_FIRST, MOD_GROUPS))
    return np.ascontiguousarray(w[order]).reshape(4 * MOD_GROUPS, P, 4, 512)


def _columns(i):
    def f(a):
        return a.reshape(-1, P).T
    qk1 = np.concatenate([np.tile(i[n][0], 2)[:, None] for n in ("att_q_norm", "att_k_norm")], axis=1)
    att_lam = np.zeros((P, 4), np.float32)
    att_lam[:HD1] = i["att_lambda"][0].T
    parts = dict(
        c=f(np.concatenate([i["c"].ravel(), i["c_ctx"], i["c_2"].ravel(), i["c_ctx_2"]])),
        norm_g=f(np.concatenate([i["norm_g"], i["norm_w_2"]])),
        mod_b=f(np.concatenate([i["mod_b"], i["b_mod_2"]])),
        conv_w=f(i["lru_conv_w"][0].reshape(4, BLOCKS, P).transpose(1, 0, 2)),
        conv_b=f(i["lru_conv_b"][0]),
        gate_b=f(i["lru_gate_b"][0].transpose(2, 0, 1, 3)),
        lam=f(i["lru_lambda"][0].reshape(2, BLOCKS, P).transpose(1, 0, 2)),
        v_norm=f(i["v_norm_w_2"]),
        qk2=f(np.concatenate([i["q_norm_w_2"], i["k_norm_w_2"]])),
        qk1=qk1, subln=f(i["att_subln"]), att_lam=att_lam)
    return np.ascontiguousarray(np.concatenate([parts[n] for n in _widths], axis=1))


def _constants():
    f = np.float32
    same = np.kron(np.eye(2), np.ones((HD1, HD1)))

    def rotation(half):
        r = np.zeros((P, P))
        for d in range(P):
            if d % (2 * half) < half:
                r[d + half, d] = -1.0
            else:
                r[d - half, d] = 1.0
        return r
    sel = np.zeros((2, P, 2))
    for net in range(2):
        for j in range(4):
            for s in range(2):
                sel[net, 32 * j + 2 * net + s, s] = 1.0
    row, colm = (np.arange(T) // 64).astype(f), (np.arange(T) % 64).astype(f)

    def tables(freqs, copies):
        inv = (f(10000.0) ** (-np.arange(freqs, dtype=f) / f(freqs))).astype(f)
        ang = np.concatenate([np.tile(pos[None, :] * inv[:, None], (2, 1)) for pos in (row, colm)])
        ang = np.tile(ang, (copies, 1)).astype(f)
        return [np.cos(ang), np.sin(ang)]
    parts = [np.eye(P), np.ones((P, P)), same, rotation(16), rotation(32), sel[0], sel[1]]
    parts += tables(16, 2) + tables(32, 1)
    return np.ascontiguousarray(np.concatenate(parts, axis=1).astype(f))


def kernel(**inputs):
    import concourse.bacc as bacc
    from concourse.bass_utils import run_bass_kernel_spmd

    i = {n: np.asarray(a) for n, a in inputs.items()}

    def feature_major(x):
        return x.reshape(T, KT, P).transpose(1, 2, 0)
    b = np.broadcast_to(i["b_sgu_2"].reshape(2 * GROUPS, 1, P), (2 * GROUPS, P, P))
    arrays = {
        "weights": _stream(i),
        "mod_weights": _mod_stream(i),
        "cols": _columns(i),
        "consts": _constants(),
        "x_t": np.ascontiguousarray(np.concatenate([feature_major(i["x"]), feature_major(i["ctx"])], axis=2)),
        "ctx2_t": np.ascontiguousarray(feature_major(i["ctx_2"])),
        "gate_w": np.ascontiguousarray(i["lru_gate_w"][0].transpose(2, 3, 0, 1, 4)).reshape(BLOCKS, P, 4 * P),
        "sgu_tab": np.ascontiguousarray(np.concatenate(
            [i["w_sgu_2"].reshape(2 * GROUPS, P, P).transpose(0, 2, 1), b], axis=2)),
    }
    nc = bacc.Bacc("TRN2", target_bir_lowering=False, num_devices=1)
    ins = {n: nc.dram_tensor("in_" + n, a.shape, mybir.dt.from_np(a.dtype), kind="ExternalInput").ap()
           for n, a in arrays.items()}
    out = nc.dram_tensor("out_t", (KT, P, T), F32, kind="ExternalOutput").ap()
    build(nc, ins, out)
    r = run_bass_kernel_spmd(nc, [{"in_" + n: a for n, a in arrays.items()}], core_ids=[0])
    return np.ascontiguousarray(r.results[0]["out_t"].transpose(2, 0, 1)).reshape(1, T, D)
```
